# Optimizing a Trainium2 kernel written in Bass

```python
import jax, jax.numpy as jnp
from jax import lax
import numpy as np

D_MODEL = 1024
BATCH = 1
SEQ = 2048
DEPTH = 2
DEC_BATCH = 8
DEC_SEQ = 1
PAST_LEN = 4096
PAGE_SIZE = 128

A_WIDTH = D_MODEL // 2
A_GROUPS = 4
A_GROUP_DIM = A_WIDTH // A_GROUPS
CHUNK = 128
B_WIDTH = D_MODEL // 2
B_BLOCKS = 8
B_BLOCK_DIM = B_WIDTH // B_BLOCKS
CONV_W = 4
LRU_C = 8.0
C_HEADS = 16
C_HEAD_DIM = D_MODEL // C_HEADS
C_WIDTH = C_HEADS * C_HEAD_DIM
Q_BLOCK = 128
ATTN_SCALE = C_HEAD_DIM ** -0.5
IN0 = 3 * A_WIDTH + 2 * B_WIDTH
IN1 = 4 * C_WIDTH + C_HEADS
EPS = 1e-6

kernel_name = "hybrid_gmlp_rglru_fox_step"

def _rmsnorm(x, g):
    xf = x.astype(jnp.float32)
    y = xf * lax.rsqrt(jnp.mean(xf * xf, axis=-1, keepdims=True) + EPS)
    return (y * g.astype(jnp.float32)).astype(x.dtype)

def _gmlp_mix(u, v, v_g, w_s, b_s):
    Bn, L, _ = v.shape
    u = jax.nn.gelu(u).reshape(Bn, L, A_GROUPS, A_GROUP_DIM)
    v = _rmsnorm(jax.nn.gelu(v).reshape(Bn, L, A_GROUPS, A_GROUP_DIM), v_g)
    pad = (-L) % CHUNK
    vp = jnp.pad(v, ((0, 0), (0, pad), (0, 0), (0, 0)))
    nc = (L + pad) // CHUNK
    vc = vp.reshape(Bn, nc, CHUNK, A_GROUPS, A_GROUP_DIM)
    causal = jnp.tril(jnp.ones((CHUNK, CHUNK), dtype=bool))
    w = jnp.where(causal[None], w_s, jnp.zeros_like(w_s))
    s = jnp.einsum('gts,bcsgd->bctgd', w, vc) + jnp.transpose(b_s)[:, :, None]
    s = s.reshape(Bn, nc * CHUNK, A_GROUPS, A_GROUP_DIM)[:, :L]
    return (u * s).reshape(Bn, L, A_WIDTH), v.reshape(Bn, L, A_WIDTH)

def _lin_combine(c1, c2):
    a1, b1 = c1
    a2, b2 = c2
    return a1 * a2, a2 * b1 + b2

def _rglru_mix(xb, conv_buf, h0, conv_w, conv_b, w_r, b_r, w_i, b_i, lam):
    Bn, L, _ = xb.shape
    xpad = jnp.concatenate([conv_buf.astype(xb.dtype), xb], axis=1)
    xc = conv_b
    for tap in range(CONV_W):
        xc = xc + conv_w[tap] * xpad[:, tap:tap + L]
    new_buf = xpad[:, L:]
    xr = xc.reshape(Bn, L, B_BLOCKS, B_BLOCK_DIM)
    r = jax.nn.sigmoid(jnp.einsum('blhi,hij->blhj', xr, w_r) + b_r).reshape(Bn, L, B_WIDTH)
    gi = jax.nn.sigmoid(jnp.einsum('blhi,hij->blhj', xr, w_i) + b_i).reshape(Bn, L, B_WIDTH)
    log_a = -LRU_C * r.astype(jnp.float32) * jax.nn.softplus(-lam.astype(jnp.float32))
    a = jnp.exp(log_a)
    bterm = jnp.sqrt(-jnp.expm1(2.0 * log_a)) * (gi * xc).astype(jnp.float32)
    bterm = bterm.at[:, 0].add(a[:, 0] * h0.astype(jnp.float32))
    _, h = lax.associative_scan(_lin_combine, (a, bterm), axis=1)
    return h.astype(xb.dtype), new_buf, h[:, -1].astype(h0.dtype)

def _layer_ab(x, conv_buf, h0, norm_g, w_in, v_g, w_s, b_s, conv_w, conv_b,
              w_r, b_r, w_i, b_i, lam, w_out):
    xn = _rmsnorm(x, norm_g)
    proj = xn @ w_in
    u, v, ga, xb, gb = jnp.split(
        proj, [A_WIDTH, 2 * A_WIDTH, 3 * A_WIDTH, 3 * A_WIDTH + B_WIDTH], axis=-1)
    a_out, v_rows = _gmlp_mix(u, v, v_g, w_s, b_s)
    b_out, new_buf, h_last = _rglru_mix(xb, conv_buf, h0, conv_w, conv_b, w_r, b_r, w_i, b_i, lam)
    mixed = jnp.concatenate([a_out * jax.nn.silu(ga), b_out * jax.nn.silu(gb)], axis=-1)
    return x + mixed @ w_out, v_rows, new_buf, h_last

def _fox_project(x, norm_g, w_in, b_f, q_g, k_g):
    Bn, L, _ = x.shape
    proj = _rmsnorm(x, norm_g) @ w_in
    q, k, v, g, f = jnp.split(proj, [C_WIDTH, 2 * C_WIDTH, 3 * C_WIDTH, 4 * C_WIDTH], axis=-1)
    q = _rmsnorm(q.reshape(Bn, L, C_HEADS, C_HEAD_DIM), q_g)
    k = _rmsnorm(k.reshape(Bn, L, C_HEADS, C_HEAD_DIM), k_g)
    v = v.reshape(Bn, L, C_HEADS, C_HEAD_DIM)
    logf = jax.nn.log_sigmoid((f + b_f).astype(jnp.float32))
    return q, k, v, g, logf

def _fox_prompt_attention(q, k, v, logf):
    Bn, L, H, hd = q.shape
    nb = L // Q_BLOCK
    ck = jnp.transpose(jnp.cumsum(logf, axis=1), (0, 2, 1))
    qb = q.reshape(Bn, nb, Q_BLOCK, H, hd).transpose(1, 0, 2, 3, 4)
    cqb = ck.reshape(Bn, H, nb, Q_BLOCK).transpose(2, 0, 1, 3)
    key_pos = jnp.arange(L)

    def one_block(args):
        q_i, cq_i, blk = args
        s = jnp.einsum('bqhd,bkhd->bhqk', q_i, k).astype(jnp.float32) * ATTN_SCALE
        s = s + cq_i[..., :, None] - ck[:, :, None, :]
        q_pos = blk * Q_BLOCK + jnp.arange(Q_BLOCK)
        mask = key_pos[None, :] <= q_pos[:, None]
        p = jax.nn.softmax(jnp.where(mask, s, -jnp.inf), axis=-1)
        return jnp.einsum('bhqk,bkhd->bqhd', p.astype(v.dtype), v)

    out = lax.map(one_block, (qb, cqb, jnp.arange(nb)))
    return out.transpose(1, 0, 2, 3, 4).reshape(Bn, L, H * hd)

def _fox_sample_attention(q, k, v, logf, past_k, past_v, past_logf):
    Bn, T, H, hd = q.shape
    P = past_k.shape[1]
    k_all = jnp.concatenate([past_k.astype(k.dtype), k], axis=1)
    v_all = jnp.concatenate([past_v.astype(v.dtype), v], axis=1)
    csum = jnp.cumsum(jnp.concatenate([past_logf.astype(jnp.float32), logf], axis=1), axis=1)
    ck = jnp.transpose(csum, (0, 2, 1))
    cq = ck[:, :, P:]
    s = jnp.einsum('bqhd,bkhd->bhqk', q, k_all).astype(jnp.float32) * ATTN_SCALE
    s = s + cq[..., :, None] - ck[:, :, None, :]
    mask = jnp.arange(P + T)[None, :] <= (P + jnp.arange(T))[:, None]
    p = jax.nn.softmax(jnp.where(mask, s, -jnp.inf), axis=-1)
    out = jnp.einsum('bhqk,bkhd->bqhd', p.astype(v_all.dtype), v_all)
    return out.reshape(Bn, T, H * hd)

def setup_inputs(seed: int = 0) -> dict:
    key = jax.random.key(seed)
    ks = jax.random.split(key, 32)
    n_pages = PAST_LEN // PAGE_SIZE
    used = DEC_BATCH * n_pages
    n_pool = used + max(1, used // 4)
    nrm = lambda k, shape, scale: jax.random.normal(k, shape, jnp.float32) * scale
    page_table = jax.random.permutation(ks[0], n_pool)[:used].reshape(DEC_BATCH, n_pages).astype(jnp.int32)
    a0 = jax.random.uniform(ks[1], (B_WIDTH,), jnp.float32, 0.9, 0.999)
    return {
        "x_prompt": nrm(ks[2], (BATCH, SEQ, D_MODEL), 1.0),
        "x_sample": nrm(ks[3], (DEC_BATCH, DEC_SEQ, D_MODEL), 1.0),
        "state_lru_conv": nrm(ks[4], (DEC_BATCH, CONV_W - 1, B_WIDTH), 1.0),
        "state_lru_h": nrm(ks[5], (DEC_BATCH, B_WIDTH), 0.5),
        "cache_k": nrm(ks[6], (n_pool, PAGE_SIZE, C_HEADS, C_HEAD_DIM), 1.0),
        "cache_v": nrm(ks[7], (n_pool, PAGE_SIZE, C_HEADS, C_HEAD_DIM), 1.0),
        "cache_logf": jax.nn.log_sigmoid(3.0 + nrm(ks[8], (n_pool, PAGE_SIZE, C_HEADS), 1.0)),
        "page_table": page_table,
        "norm0_g": 1.0 + nrm(ks[9], (D_MODEL,), 0.02),
        "w_in0": nrm(ks[10], (D_MODEL, IN0), D_MODEL ** -0.5),
        "gmlp_v_g": 1.0 + nrm(ks[11], (A_GROUPS, A_GROUP_DIM), 0.02),
        "gmlp_w_s": nrm(ks[12], (A_GROUPS, CHUNK, CHUNK), CHUNK ** -0.5),
        "gmlp_b_s": 1.0 + nrm(ks[13], (A_GROUPS, CHUNK), 0.02),
        "lru_conv_w": nrm(ks[14], (CONV_W, B_WIDTH), CONV_W ** -0.5),
        "lru_conv_b": nrm(ks[15], (B_WIDTH,), 0.02),
        "lru_w_r": nrm(ks[16], (B_BLOCKS, B_BLOCK_DIM, B_BLOCK_DIM), B_BLOCK_DIM ** -0.5),
        "lru_b_r": nrm(ks[17], (B_BLOCKS, B_BLOCK_DIM), 0.02),
        "lru_w_i": nrm(ks[18], (B_BLOCKS, B_BLOCK_DIM, B_BLOCK_DIM), B_BLOCK_DIM ** -0.5),
        "lru_b_i": nrm(ks[19], (B_BLOCKS, B_BLOCK_DIM), 0.02),
        "lru_lambda": jnp.log(a0) - jnp.log1p(-a0),
        "w_out0": nrm(ks[20], (A_WIDTH + B_WIDTH, D_MODEL), (A_WIDTH + B_WIDTH) ** -0.5),
        "norm1_g": 1.0 + nrm(ks[21], (D_MODEL,), 0.02),
        "w_in1": nrm(ks[22], (D_MODEL, IN1), D_MODEL ** -0.5),
        "fox_b_f": 3.0 + nrm(ks[23], (C_HEADS,), 0.1),
        "q_norm_g": 1.0 + nrm(ks[24], (C_HEAD_DIM,), 0.02),
        "k_norm_g": 1.0 + nrm(ks[25], (C_HEAD_DIM,), 0.02),
        "w_out1": nrm(ks[26], (C_WIDTH, D_MODEL), C_WIDTH ** -0.5),
    }

def reference(x_prompt, x_sample, state_lru_conv, state_lru_h, cache_k, cache_v, cache_logf,
              page_table, norm0_g, w_in0, gmlp_v_g, gmlp_w_s, gmlp_b_s, lru_conv_w, lru_conv_b,
              lru_w_r, lru_b_r, lru_w_i, lru_b_i, lru_lambda, w_out0, norm1_g, w_in1, fox_b_f,
              q_norm_g, k_norm_g, w_out1):
    yp, ys = x_prompt, x_sample
    Bp = x_prompt.shape[0]
    Bs = x_sample.shape[0]
    for layer in range(DEPTH):
        if layer % 2 == 0:
            ab_params = (norm0_g, w_in0, gmlp_v_g, gmlp_w_s, gmlp_b_s, lru_conv_w, lru_conv_b,
                         lru_w_r, lru_b_r, lru_w_i, lru_b_i, lru_lambda, w_out0)
            conv0 = jnp.zeros((Bp, CONV_W - 1, B_WIDTH), yp.dtype)
            h0 = jnp.zeros((Bp, B_WIDTH), yp.dtype)
            yp, _, lru_conv_p, lru_h_p = _layer_ab(yp, conv0, h0, *ab_params)
            ys, gmlp_v_s, lru_conv_s, lru_h_s = _layer_ab(ys, state_lru_conv, state_lru_h, *ab_params)
        else:
            q, k_p, v_p, g, logf_p = _fox_project(yp, norm1_g, w_in1, fox_b_f, q_norm_g, k_norm_g)
            att = _fox_prompt_attention(q, k_p, v_p, logf_p)
            yp = yp + (att * jax.nn.silu(g)) @ w_out1
            q, k_s, v_s, g, logf_s = _fox_project(ys, norm1_g, w_in1, fox_b_f, q_norm_g, k_norm_g)
            past_k = cache_k[page_table].reshape(Bs, -1, C_HEADS, C_HEAD_DIM)
            past_v = cache_v[page_table].reshape(Bs, -1, C_HEADS, C_HEAD_DIM)
            past_logf = cache_logf[page_table].reshape(Bs, -1, C_HEADS)
            att = _fox_sample_attention(q, k_s, v_s, logf_s, past_k, past_v, past_logf)
            ys = ys + (att * jax.nn.silu(g)) @ w_out1
    return (yp, ys, lru_conv_p, lru_h_p, k_p, v_p, logf_p,
            gmlp_v_s, lru_conv_s, lru_h_s, k_s, v_s, logf_s)


_drawn_inputs = setup_inputs


def setup_inputs(seed=0):
    import zlib

    import numpy as np

    out = dict(_drawn_inputs(seed))
    spreads = {}
    factors = {'gmlp_v_g': 2.724,
     'gmlp_b_s': 8.0,
     'lru_b_r': 8.0,
     'lru_b_i': 6.424,
     'norm1_g': 2.727,
     'q_norm_g': 8.0,
     'k_norm_g': 2.872}
    for name, (base, spread) in spreads.items():
        noise = np.random.default_rng([zlib.crc32(name.encode()), seed]).standard_normal(out[name].shape)
        drawn = base * np.exp(spread * noise) if base else spread * noise
        out[name] = __import__('jax').numpy.asarray(drawn.astype(out[name].dtype))
    for name, factor in factors.items():
        out[name] = (out[name] * factor).astype(out[name].dtype)
    return out
```

```python
import concourse.bass as bass
from concourse import mybir
from contextlib import ExitStack

F32 = mybir.dt.float32
F32R = mybir.dt.float32r
U32 = mybir.dt.uint32
I32 = mybir.dt.int32
ACT = mybir.ActivationFunctionType
ALU = mybir.AluOpType
AX = mybir.AxisListType
ds = bass.ds

P = 128
EPS = 1e-6
LRU_C = 8.0
NEG = -1.0e30


class Shapes:

    def __init__(s, a):
        _, s.T, s.D = a["x_prompt"].shape
        s.B = a["x_sample"].shape[0]
        s.KB = s.D // P
        s.AW = s.D // 2
        s.G = s.AW // P
        s.H, s.HD = a["cache_k"].shape[2], a["cache_k"].shape[3]
        s.POOL = a["cache_k"].shape[0]
        s.PG = a["page_table"].shape[1]
        s.NT = s.T // P
        s.TS = s.T + s.B
        s.NCH = -(-s.TS // 512)
        s.CW = -(-s.TS // (2 * s.NCH)) * 2
        s.TP = s.NCH * s.CW
        s.NQ = s.NT // 4
        s.PAIRS = s.H // 2
        s.TAPS = a["lru_conv_w"].shape[0]
        s.SB = min(s.B * s.PG, P) // s.PG
        s.GP = s.SB * s.PG
        s.PX = s.PG + 1
        assert s.B == s.PAIRS and s.NT % 4 == 0 and s.PG % 4 == 0 and s.HD * 2 == P and s.B % s.SB == 0


class Stage:

    def __init__(s, nc, ctx, name):
        s.nc, s.ctx, s.name, s.used = nc, ctx, name, []
        ctx.callback(s.end)

    def end(s):
        if s.used:
            s.nc.clear_and_free_semaphores(s.used)
            s.nc.all_engine_barrier()

    def sb(s, n, shape, dt=F32):
        return s.ctx.enter_context(s.nc.sbuf_tensor(f"{s.name}_{n}", shape, dt))

    def ps(s, n, shape):
        return s.ctx.enter_context(s.nc.psum_tensor(f"{s.name}_{n}", shape, F32))

    def sem(s, n):
        s.used.append(s.nc.alloc_semaphore(name=f"{s.name}_{n}"))
        return s.used[-1]

    def sems(s, names):
        return [s.sem(n) for n in names.split()]


def wait_apart(eng, sem, value, met, n):
    v = eng.snap(value)
    eng.wait_ge(met, n)
    eng.wait_ge(sem, v)
    eng.nop(nofuse=True)


def each(eng, n, body):
    body(0)
    with eng.Fori(1, n) as i:
        body(i)


def split3(nc, out, lhs, rhs, k, nk):
    nc.tensor.matmul(out, lhs[0], rhs[0], start=(k == 0), stop=False)
    nc.tensor.matmul(out, lhs[0], rhs[1], start=False, stop=False)
    return nc.tensor.matmul(out, lhs[1], rhs[0], start=False, stop=(k == nk - 1))


def setup(nc, z, a, C):
    with ExitStack() as ctx:
        S = Stage(nc, ctx, "su")
        ws = S.sb("ws", [P, z.G, P])
        st = S.sb("st", [3 * z.B, z.AW])
        sh = S.sb("sh", [z.B, z.AW])
        w00 = S.sb("w00", [z.B, z.G])
        lam = S.sb("lam", [P, z.G])
        t1 = S.sb("t1", [P, z.G])
        ps = S.ps("ps", [P, 3, 512])
        loaded, filled, picked, turned, copied, wmask, lnd, dv = S.sems("loaded filled picked turned copied wmask lnd dv")
        loads = [
            (ws[:], a["gmlp_w_s"].rearrange("g t s -> t g s")),
            (st[:], a["state_lru_conv"].rearrange("b k c -> (b k) c")),
            (sh[:], a["state_lru_h"]),
            (lam[:], a["lru_lambda"].rearrange("(g p) -> p g", p=P)),
            (C.gv[:], a["gmlp_v_g"].rearrange("g d -> (g d)").partition_broadcast(P)),
            (C.bs[:], a["gmlp_b_s"].rearrange("g d -> (g d)").partition_broadcast(P)),
            (C.convb[:], a["lru_conv_b"].rearrange("(g p) -> p g", p=P)),
            (C.br[:], a["lru_b_r"].rearrange("(g x) j -> (x j) g", x=2)),
            (C.bi[:], a["lru_b_i"].rearrange("(g x) j -> (x j) g", x=2)),
            (C.bf[:], a["fox_b_f"].rearrange("(h o) -> h o", o=1)),
        ] + [(w00[b:b + 1, :], a["gmlp_w_s"][:, 0, 0:1].rearrange("g o -> o g")) for b in range(z.B)] \
          + [(C.convw[:, :, k], a["lru_conv_w"][k].rearrange("(g p) -> p g", p=P)) for k in range(z.TAPS)] \
          + [(C.qg[x * z.HD:(x + 1) * z.HD, :], a["q_norm_g"].rearrange("(d o) -> d o", o=1)) for x in range(2)] \
          + [(C.kg[x * z.HD:(x + 1) * z.HD, :], a["k_norm_g"].rearrange("(d o) -> d o", o=1)) for x in range(2)]
        block = ctx.enter_context(nc.Block())

        @block.sync
        def _(sp):
            for dst, src in loads:
                sp.dma_start(dst, src).then_inc(loaded, 16)
            sp.wait_ge(loaded, 16 * len(loads))

        @block.gpsimd
        def _(pool):
            fills = [(C.ident, 0.0), (C.pairsum, 0.0), (C.onescol, 1.0), (C.eps, EPS)]
            for t, v in fills:
                nc.gpsimd.memset(t[:], v).then_inc(filled, 1)
            pool.wait_ge(filled, len(fills))
            nc.gpsimd.affine_select(out=C.ident[:], in_=C.ident[:], compare_op=ALU.not_equal, fill=1.0, base=0,
                                    pattern=[[-1, P]], channel_multiplier=1).then_inc(picked, 1)
            for x in range(2):
                pool.wait_ge(picked, 1 + x)
                nc.gpsimd.memset(C.pairsum[x * z.HD:(x + 1) * z.HD, x * z.HD:(x + 1) * z.HD], 1.0).then_inc(picked, 1)
            pool.wait_ge(picked, 3)
            pool.wait_ge(copied, 1)
            nc.gpsimd.affine_select(out=C.wst[:], in_=C.wst[:], compare_op=ALU.is_ge, fill=0.0, base=0,
                                    pattern=[[0, z.G], [1, P]], channel_multiplier=-1).then_inc(wmask, 1)
            pool.wait_ge(wmask, 1)

        @block.tensor
        def _(pe):
            pe.wait_ge(loaded, 16 * len(loads))
            pe.wait_ge(picked, 1)
            for g in range(z.G):
                nc.tensor.transpose(ps[:, 0, g * P:(g + 1) * P], ws[:, g, :], C.ident[:])
            for g in range(z.G):
                nc.tensor.transpose(ps[:, 1, g * 3 * z.B:(g + 1) * 3 * z.B], st[:, g * P:(g + 1) * P],
                                    C.ident[0:3 * z.B, 0:3 * z.B])
            for g in range(z.G):
                last = nc.tensor.transpose(ps[:, 2, g * z.B:(g + 1) * z.B], sh[:, g * P:(g + 1) * P],
                                           C.ident[0:z.B, 0:z.B])
            last.then_inc(turned, 1)

        @block.scalar
        def _(act):
            act.wait_ge(loaded, 16 * len(loads))
            nc.scalar.activation(t1[:], lam[:], ACT.Abs).then_inc(lnd, 1)
            act.wait_ge(lnd, 1)
            nc.scalar.activation(t1[:], t1[:], ACT.Exp, scale=-1.0).then_inc(lnd, 1)
            act.wait_ge(lnd, 2)
            nc.scalar.activation(t1[:], t1[:], ACT.Ln, bias=1.0).then_inc(lnd, 1)

        @block.vector
        def _(dve):
            dve.wait_ge(turned, 1)
            nc.vector.tensor_copy(C.wst[:].rearrange("p g t -> p (g t)"), ps[:, 0, 0:z.G * P]).then_inc(copied, 1)
            nc.vector.tensor_copy(C.stc[:].rearrange("p g r -> p (g r)"), ps[:, 1, 0:z.G * 3 * z.B]).then_inc(dv, 1)
            nc.vector.tensor_copy(C.h0[:].rearrange("p g b -> p (g b)"), ps[:, 2, 0:z.G * z.B]).then_inc(dv, 1)
            dve.wait_ge(loaded, 16 * len(loads))
            dve.wait_ge(picked, 1)
            for g in range(z.G):
                nc.vector.tensor_scalar(C.w00[:, g, :], C.ident[0:z.B, 0:z.B], w00[:, g:g + 1], None,
                                        ALU.mult).then_inc(dv, 1)
            nc.vector.tensor_scalar(C.qg[:], C.qg[:], z.HD ** -0.5, None, ALU.mult).then_inc(dv, 1)
            dve.wait_ge(lnd, 3)
            nc.vector.tensor_scalar(C.lsc[:], lam[:], -1.0, 0.0, ALU.mult, ALU.max).then_inc(dv, 1)
            dve.wait_ge(dv, 4 + z.G)
            nc.vector.tensor_tensor(C.lsc[:], C.lsc[:], t1[:], ALU.add).then_inc(dv, 1)
            dve.wait_ge(dv, 5 + z.G)
            nc.vector.tensor_scalar(C.lsc[:], C.lsc[:], -LRU_C, None, ALU.mult).then_inc(dv, 1)
            dve.wait_ge(dv, 6 + z.G)


def tiles_stage(nc, z, C, name, x_of, norm_g=None, xh=None, xl=None, mix=None, w_out=None, x_out=None, lsum=None):
    with ExitStack() as ctx:
        S = Stage(nc, ctx, name)
        proj, norm = mix is not None, norm_g is not None
        xt = S.sb("x", [P, 2, z.D])
        x_in = S.sems("x_in0 x_in1")
        (x1d, sqd, stdd, rcd, xnd, trd, hid, lod, prd, mxd, rbd, rl, padded) = S.sems(
            "x1 squared std rstd xn turned hi lo product mixed spread rl padded")
        w_in, m_in, l_in = S.sem("w_in"), S.sems("m_in0 m_in1"), S.sem("l_in")
        x_st = S.sems("x_st0 x_st1")
        g_in, exd = S.sems("g_in expanded")
        if norm:
            gb = S.sb("gb", [P, z.D])
            sq = S.sb("sq", [P, z.D])
            st = S.sb("st", [P, 2, 3])
            xn = S.sb("xn", [P, 2, z.D])
            tp = S.ps("tp", [P, 2, z.KB, P])
        if proj:
            wo = S.sb("wo", [P, z.KB, z.D])
            mt = S.sb("mt", [P, 2, z.KB, P])
            pp = S.ps("pp", [P, 2, z.D])
        if lsum is not None:
            md = S.sb("md", [P, 2, z.KB, P])
            ls = S.sb("ls", [z.H, z.TS])
            expand = S.sb("expand", [z.H, z.D])
            rb = S.ps("rb", [P, 2, z.KB, P])
        block = ctx.enter_context(nc.Block())
        lhs = md if lsum is not None else (mt if proj else None)

        def steps(eng, step):
            step(0, 0, P, 0, True)
            step(1, 1, P, P, False)
            if z.NT > 2:
                with eng.Fori(1, z.NT // 2) as i:
                    for s in range(2):
                        step(2 * i + s, s, P, (2 * i + s) * P, None)
            step(z.NT, 0, z.B, z.T, None)


        @block.sync
        def _(sp):
            if norm:
                sp.dma_start(gb[:], norm_g.partition_broadcast(P)).then_inc(g_in, 16)
            if proj:
                sp.dma_start(wo[:], w_out.rearrange("(k p) n -> p k n", p=P)).then_inc(w_in, 16)
            if lsum is not None:
                sp.dma_start(ls[:], lsum).then_inc(l_in, 16)

            def load(n, s, rows, col, first):
                if first is None:
                    if norm:
                        wait_apart(sp, xnd, n - 1, x_in[0], 16)
                    if x_out is not None:
                        wait_apart(sp, x_st[s], 8 * (n - s), x_in[0], 16)
                if proj:
                    if first is None:
                        sp.wait_ge(mxd if lsum is not None else prd, n - 1)
                    sp.dma_start(mt[:, s, :, 0:rows],
                                 mix[:, ds(col, rows)].rearrange("(k p) t -> p k t", p=P)).then_inc(m_in[s], 16)
                sp.dma_start(xt[0:rows, s, :], x_of(col, rows)).then_inc(x_in[s], 16)

            def store(n, s, rows, col):
                sp.wait_ge(x1d, n + 1)
                sp.dma_start(x_out(col, rows), xt[0:rows, s, :]).then_inc(x_st[s], 16)

            if x_out is None:
                steps(sp, load)
            else:
                load(0, 0, P, 0, True)
                load(1, 1, P, P, False)
                store(0, 0, P, 0)
                with sp.Fori(1, z.NT // 2) as i:
                    load(2 * i, 0, P, 2 * i * P, None)
                    store(2 * i - 1, 1, P, (2 * i - 1) * P)
                    load(2 * i + 1, 1, P, (2 * i + 1) * P, None)
                    store(2 * i, 0, P, 2 * i * P)
                load(z.NT, 0, z.B, z.T, None)
                store(z.NT - 1, 1, P, (z.NT - 1) * P)
                store(z.NT, 0, z.B, z.T)
                sp.wait_ge(x_st[0], 16 * (z.NT // 2 + 1))
                sp.wait_ge(x_st[1], 16 * (z.NT // 2))

        @block.scalar
        def _(act):
            def hi(n, s, rows, col):
                act.wait_ge(trd, n + 1)
                nc.scalar.activation(xh[:, :, ds(col, rows)], tp[:, s, :, 0:rows], ACT.Copy).then_inc(hid, 1)

            def step(n, s, rows, col, first):
                if proj:
                    act.wait_ge(x1d, n + 1)
                else:
                    act.wait_ge(x_in[s], 8 * (n - s) + 16)
                nc.scalar.activation(sq[0:rows], xt[0:rows, s, :], ACT.Square,
                                     accum_out=st[0:rows, s, 0:1]).then_inc(sqd, 1)
                act.wait_ge(sqd, n + 1)
                nc.scalar.activation(st[0:rows, s, 1:2], st[0:rows, s, 0:1], ACT.Sqrt, scale=1.0 / z.D,
                                     bias=C.eps[0:rows]).then_inc(stdd, 1)
                if first is not True:
                    hi(n - 1, 1 - s, P, col - P)

            if norm:
                steps(act, step)
                hi(z.NT, 0, z.B, z.T)

        @block.gpsimd
        def _(pool):
            if norm and z.TP > z.TS:
                nc.gpsimd.memset(xh[:, :, z.TS:z.TP].bitcast(F32), 0.0).then_inc(padded, 1)
                nc.gpsimd.memset(xl[:, :, z.TS:z.TP].bitcast(F32), 0.0).then_inc(padded, 1)
                pool.wait_ge(padded, 2)
            if lsum is not None:
                nc.gpsimd.memset(expand[:], 1.0).then_inc(exd, 1)
                pool.wait_ge(exd, 1)
                nc.gpsimd.affine_select(out=expand[:], in_=expand[:], compare_op=ALU.is_ge, fill=0.0, base=0,
                                        pattern=[[1, z.D]], channel_multiplier=-z.HD).then_inc(exd, 1)
                pool.wait_ge(exd, 2)
                nc.gpsimd.affine_select(out=expand[:], in_=expand[:], compare_op=ALU.is_ge, fill=0.0, base=z.HD - 1,
                                        pattern=[[-1, z.D]], channel_multiplier=z.HD).then_inc(exd, 1)

        @block.vector
        def _(dve):
            def lo(n, s, rows, col):
                dve.wait_ge(hid, n + 1)
                nc.vector.tensor_tensor(xl[:, :, ds(col, rows)], tp[:, s, :, 0:rows],
                                        xh[:, :, ds(col, rows)].bitcast(F32), ALU.subtract).then_inc(lod, 1)

            def divide(n, s, rows, first):
                dve.wait_ge(rbd, n + 1)
                dve.wait_ge(m_in[s], 8 * (n - s) + 16)
                if first is None:
                    dve.wait_ge(prd, n - 1)
                nc.vector.tensor_tensor(md[:, s, :, 0:rows], mt[:, s, :, 0:rows], rb[:, s, :, 0:rows],
                                        ALU.mult).then_inc(mxd, 1)

            def step(n, s, rows, col, first):
                if lsum is not None:
                    divide(n, s, rows, first)
                dve.wait_ge(x_in[s], 8 * (n - s) + 16)
                if proj:
                    dve.wait_ge(prd, n + 1)
                    nc.vector.tensor_tensor(xt[0:rows, s, :], xt[0:rows, s, :], pp[0:rows, s, :],
                                            ALU.add).then_inc(x1d, 1)
                if norm:
                    dve.wait_ge(stdd, n + 1)
                    nc.vector.reciprocal(st[0:rows, s, 2:3], st[0:rows, s, 1:2]).then_inc(rcd, 1)
                    dve.wait_ge(rcd, n + 1)
                    if first is None:
                        dve.wait_ge(trd, n - 1)
                    nc.vector.scalar_tensor_tensor(out=xn[0:rows, s, :], in0=xt[0:rows, s, :], scalar=st[0:rows, s, 2:3],
                                                   in1=gb[0:rows], op0=ALU.mult, op1=ALU.mult).then_inc(xnd, 1)
                    if first is not True:
                        lo(n - 1, 1 - s, P, col - P)

            if lsum is not None:
                dve.wait_ge(l_in, 16)
                nc.vector.reciprocal(ls[:], ls[:]).then_inc(rl, 1)
            if norm:
                dve.wait_ge(g_in, 16)
            steps(dve, step)
            if norm:
                lo(z.NT, 0, z.B, z.T)

        @block.tensor
        def _(pe):
            def turn(n, s, rows, first):
                pe.wait_ge(xnd, n + 1)
                if first is None:
                    pe.wait_ge(lod, n - 1)
                for k in range(z.KB):
                    last = nc.tensor.transpose(tp[:, s, k, 0:rows], xn[0:rows, s, k * P:(k + 1) * P],
                                               C.ident[0:rows, 0:rows])
                last.then_inc(trd, 1)

            def spread(n, s, rows, col, first):
                if first is None:
                    pe.wait_ge(mxd, n - 1)
                for k in range(z.KB):
                    last = nc.tensor.matmul(rb[:, s, k, 0:rows], expand[:, k * P:(k + 1) * P],
                                            ls[:, ds(col, rows)], start=True, stop=True)
                last.then_inc(rbd, 1)

            def product(n, s, rows, first):
                if lsum is not None:
                    pe.wait_ge(mxd, n + 1)
                else:
                    pe.wait_ge(m_in[s], 8 * (n - s) + 16)
                if first is None:
                    pe.wait_ge(x1d, n - 1)
                for half in range(z.D // 512):
                    cols = slice(half * 512, half * 512 + 512)
                    for k in range(z.KB):
                        last = nc.tensor.matmul(pp[0:rows, s, cols], lhs[:, s, k, 0:rows], wo[:, k, cols],
                                                start=(k == 0), stop=(k == z.KB - 1))
                last.then_inc(prd, 1)

            def step(n, s, rows, col, first):
                if proj:
                    if lsum is not None:
                        spread(n, s, rows, col, first)
                    product(n, s, rows, first)
                    if norm and first is not True:
                        turn(n - 1, 1 - s, P, None if first is None else True)
                else:
                    turn(n, s, rows, first)

            if proj:
                pe.wait_ge(w_in, 16)
            if lsum is not None:
                pe.wait_ge(rl, 1)
                pe.wait_ge(exd, 3)
            if proj and norm:
                product(0, 0, P, True)
                product(1, 1, P, False)
                turn(0, 0, P, True)
                product(2, 0, P, None)
                turn(1, 1, P, False)
                product(3, 1, P, None)
                turn(2, 0, P, None)
                with pe.Fori(2, z.NT // 2) if z.NT > 4 else ExitStack() as i:
                    if z.NT > 4:
                        product(2 * i, 0, P, None)
                        turn(2 * i - 1, 1, P, None)
                        product(2 * i + 1, 1, P, None)
                        turn(2 * i, 0, P, None)
                product(z.NT, 0, z.B, None)
                turn(z.NT - 1, 1, P, None)
                turn(z.NT, 0, z.B, None)
            else:
                steps(pe, step)


def layer0(nc, z, a, C, xh, xl, mixed, out):
    TILES = 5
    cols = [z.AW, 0, 2 * z.AW, 3 * z.AW, 4 * z.AW]
    wslot = [j % 2 for j in range(TILES)]
    T, TS, TP, CW, NCH = z.T, z.TS, z.TP, z.CW, z.NCH
    WW = TP + z.TAPS - 1
    with ExitStack() as ctx:
        S = Stage(nc, ctx, "l0")
        raw = S.sb("raw", [P, z.KB, P])
        wh = S.sb("wh", [P, 2, z.KB, P], F32R)
        wl = S.sb("wl", [P, 2, z.KB, P], F32R)
        W = [S.sb(f"w{x}", [P, WW if x == 3 else TP]) for x in range(5)]
        tmp = S.sb("tmp", [P, 512])
        vs = S.sb("vs", [z.B, P])
        ss = S.sb("ss", [P, z.NT + 1, 3])
        wr = S.sb("wr", [P, P])
        wi = S.sb("wi", [P, P])
        keep = S.sb("keep", [P, 2, z.G, z.TAPS - 1 + z.B])
        rows = S.sb("rows", [z.TAPS - 1 + z.B, 2, z.AW])
        pb = [S.ps(f"pb{c}", [P, 512]) for c in range(NCH)]
        px = [S.ps(f"px{c}", [P, 512]) for c in range(3)]
        (raw_in, hi, lo, proj, evac, vturn, vcopy, vsq, vstd, vready, sturn, sread, amix, ast) = S.sems(
            "raw_in hi lo projected evacuated vturned vcopied vsquared vstd vready mixed_s s_read a_mixed a_stored")
        (zeroed, xcready, gate, gated, aexp, th, bpre, bsq, bst, bready, wz, wg_in, conv, dv, kept, kturn, kcopy, kst, vst) = S.sems(
            "zeroed xc_ready gate_product gated a_exp tanh b_pre b_sqrt b_stored b_ready wz wg_in conv dv kept kturned kcopied kstored vs_stored")
        QT = z.NQ + 1
        block = ctx.enter_context(nc.Block())

        @block.sync
        def _(sp):
            def chunk(g):
                for j in range(TILES):
                    wait_apart(sp, lo, TILES * g + j, wz, 2)
                    sp.dma_start(raw[:], a["w_in0"][:, ds(cols[j] + P * g, P)].rearrange("(k p) n -> p k n", p=P)).then_inc(raw_in, 16)
                    if j == 0:
                        sp.wait_ge(wz, 2)
                        sp.wait_ge(gated, 2 * NCH * g)
                        for x in range(2):
                            d = slice(64 * x, 64 * x + 64)
                            sp.dma_start(wr[d, d], a["lru_w_r"][ds(2 * g + x, 1)].rearrange("o i j -> (o i) j")).then_inc(wg_in, 16)
                            sp.dma_start(wi[d, d], a["lru_w_i"][ds(2 * g + x, 1)].rearrange("o i j -> (o i) j")).then_inc(wg_in, 16)

            each(sp, z.G, chunk)

        @block.gpsimd
        def _(pool):
            nc.gpsimd.memset(wr[:], 0.0).then_inc(wz, 1)
            nc.gpsimd.memset(wi[:], 0.0).then_inc(wz, 1)
            K = z.TAPS - 1
            pool.dma_start(out["lru_conv_sample"][:, 0:K - 1, :], a["state_lru_conv"][:, 1:K, :]).then_inc(kst, 16)
            def chunk(g):
                wait_apart(pool, vready, 2 * g + 2, wz, 2)
                pool.dma_start(out["gmlp_v_sample"][:, 0, ds(P * g, P)], vs[:]).then_inc(vst, 16)
                wait_apart(pool, amix, QT * g + QT, wz, 2)
                pool.dma_start(mixed[ds(P * g, P), 0:TS], W[1][:, 0:TS]).then_inc(ast, 16)
                wait_apart(pool, bready, g + 1, wz, 2)
                pool.dma_start(mixed[ds(z.AW + P * g, P), 0:TS], W[1][:, 0:TS]).then_inc(bst, 16)

            each(pool, z.G, chunk)
            pool.wait_ge(kcopy, 2)
            pool.dma_start(out["lru_conv_prompt"][0], rows[0:K, 0, :]).then_inc(kst, 16)
            pool.dma_start(out["lru_conv_sample"][:, K - 1, :], rows[K:K + z.B, 0, :]).then_inc(kst, 16)
            pool.dma_start(out["lru_h_prompt"], rows[K - 1:K, 1, :]).then_inc(kst, 16)
            pool.dma_start(out["lru_h_sample"], rows[K:K + z.B, 1, :]).then_inc(kst, 16)
            pool.wait_ge(kst, 16 * 5)
            pool.wait_ge(vst, 16 * z.G)
            pool.wait_ge(ast, 16 * z.G)
            pool.wait_ge(bst, 16 * z.G)

        @block.tensor
        def _(pe):
            def project(g, j):
                s = wslot[j]
                pe.wait_ge(lo, TILES * g + j + 1)
                for c in range(NCH):
                    pe.wait_ge(evac, TILES * NCH * g if j == 0 else (TILES * g + j - 1) * NCH + c + 1)
                    for k in range(z.KB):
                        last = split3(nc, pb[c][:, 0:CW], (wh[:, s, k, :], wl[:, s, k, :]),
                                      (xh[:, k, c * CW:(c + 1) * CW], xl[:, k, c * CW:(c + 1) * CW]), k, z.KB)
                    last.then_inc(proj, 1)

            def chunk(g):
                project(g, 0)
                project(g, 1)
                pe.wait_ge(evac, (TILES * g + 1) * NCH)
                pe.wait_ge(gated, 2 * NCH * g)
                for q in range(QT):
                    if q >= 2:
                        pe.wait_ge(vcopy, QT * g + q - 1)
                    for t in range(4 if q < z.NQ else 1):
                        n = P if q < z.NQ else z.B
                        col = (4 * q + t) * P
                        last = nc.tensor.transpose(px[q % 2][0:n, t * P:(t + 1) * P], W[0][:, col:col + n], C.ident[:])
                    last.then_inc(vturn, 1)
                project(g, 2)
                pe.wait_ge(vready, 2 * g + 2)
                for q in range(QT):
                    if q >= 2:
                        pe.wait_ge(sread, QT * g + q - 1)
                    b = px[2 - q % 2]
                    if q < z.NQ:
                        for t in range(4):
                            col = (4 * q + t) * P
                            last = nc.tensor.matmul(b[:, t * P:(t + 1) * P], W[3][:, col:col + P],
                                                    C.wst[:, ds(g, 1), :].rearrange("p o t -> p (o t)"), start=True, stop=True)
                    else:
                        last = nc.tensor.matmul(b[:, 0:z.B], vs[:], C.w00[:, ds(g, 1), :].rearrange("p o t -> p (o t)"),
                                                start=True, stop=True)
                    last.then_inc(sturn, 1)
                project(g, 3)
                project(g, 4)
                pe.wait_ge(xcready, g + 1)
                pe.wait_ge(wg_in, 64 * g + 64)
                for c in range(NCH):
                    for x, w in enumerate((wr, wi)):
                        m = 2 * c + x
                        if m >= 2:
                            pe.wait_ge(gated, 2 * NCH * g + m - 1)
                        nc.tensor.matmul(px[m % 2][:, 0:CW], w[:], W[4][:, c * CW:(c + 1) * CW],
                                         start=True, stop=True).then_inc(gate, 1)

            each(pe, z.G, chunk)
            pe.wait_ge(kept, 2 * z.G)
            pe.wait_ge(gated, 2 * NCH * z.G)
            for x in range(2):
                for g in range(z.G):
                    last = nc.tensor.transpose(px[x][0:z.TAPS - 1 + z.B, g * P:(g + 1) * P], keep[:, x, g, :], C.ident[:])
                last.then_inc(kturn, 1)

        @block.scalar
        def _(act):
            def split_hi(g, j):
                act.wait_ge(raw_in, 16 * (TILES * g + j + 1))
                act.wait_ge(proj, TILES * NCH * g if j < 2 else (TILES * g + j - 1) * NCH)
                nc.scalar.activation(wh[:, wslot[j]], raw[:], ACT.Copy).then_inc(hi, 1)

            def evacuate(g, j, dst, func, off=0):
                for c in range(NCH):
                    act.wait_ge(proj, (TILES * g + j) * NCH + c + 1)
                    nc.scalar.activation(dst[:, off + c * CW:off + (c + 1) * CW], pb[c][:, 0:CW], func).then_inc(evac, 1)

            def chunk(g):
                split_hi(g, 0)
                split_hi(g, 1)
                act.wait_ge(bready, g)
                evacuate(g, 0, W[0], ACT.Gelu_apprx_tanh)
                split_hi(g, 2)
                act.wait_ge(bst, 16 * g)
                evacuate(g, 1, W[1], ACT.Gelu_apprx_tanh)
                split_hi(g, 3)
                for q in range(QT):
                    act.wait_ge(vcopy, QT * g + q + 1)
                    for t in range(4 if q < z.NQ else 1):
                        n = P if q < z.NQ else z.B
                        rowsq = W[3][:, (4 * q + t) * P:(4 * q + t + 1) * P] if q < z.NQ else vs[:]
                        nc.scalar.activation(W[2][0:n, 0:P], rowsq, ACT.Square,
                                             accum_out=ss[0:n, 4 * q + t, 0:1]).then_inc(vsq, 1)
                        act.wait_ge(vsq, (z.NT + 1) * g + 4 * q + t + 1)
                nc.scalar.activation(ss[:, 0:z.NT, 1], ss[:, 0:z.NT, 0], ACT.Sqrt, scale=1.0 / P, bias=C.eps[:]).then_inc(vstd, 1)
                nc.scalar.activation(ss[0:z.B, z.NT, 1:2], ss[0:z.B, z.NT, 0:1], ACT.Sqrt, scale=1.0 / P,
                                     bias=C.eps[0:z.B]).then_inc(vstd, 1)
                evacuate(g, 2, W[2], ACT.Silu)
                split_hi(g, 4)
                act.wait_ge(zeroed, g + 1)
                evacuate(g, 3, W[3], ACT.Copy, z.TAPS - 1)
                act.wait_ge(ast, 16 * g + 16)
                evacuate(g, 4, W[1], ACT.Silu)
                for c in range(NCH):
                    for x, (dst, b) in enumerate(((W[0], C.br), (W[2], C.bi))):
                        m = 2 * c + x
                        wait_apart(act, gate, 2 * NCH * g + m + 1, raw_in, 16)
                        nc.scalar.activation(dst[:, c * CW:(c + 1) * CW], px[m % 2][:, 0:CW], ACT.Sigmoid,
                                             bias=b[:, ds(g, 1)]).then_inc(gated, 1)
                wait_apart(act, gated, 2 * NCH * g + 2 * NCH, raw_in, 16)
                wait_apart(act, kept, 2 * g + 1, raw_in, 16)
                nc.scalar.activation(W[3][:, 0:TP], W[0][:], ACT.Exp, scale=C.lsc[:, ds(g, 1)]).then_inc(aexp, 1)
                wait_apart(act, aexp, g + 1, raw_in, 16)
                nc.scalar.activation(W[0][:], W[0][:], ACT.Tanh, scale=C.lsc[:, ds(g, 1)]).then_inc(th, 1)
                act.wait_ge(bpre, g + 1)
                nc.scalar.activation(W[4][:], W[4][:], ACT.Sqrt, scale=-1.0).then_inc(bsq, 1)

            each(act, z.G, chunk)

        @block.vector
        def _(dve):
            def split_lo(g, j):
                dve.wait_ge(hi, TILES * g + j + 1)
                nc.vector.tensor_tensor(wl[:, wslot[j]], raw[:], wh[:, wslot[j]].bitcast(F32), ALU.subtract).then_inc(lo, 1)

            chain = [0]

            def then(g, ins, total):
                chain[0] += 1
                ins.then_inc(dv, 1)
                dve.wait_ge(dv, total * g + chain[0])

            CH = 16
            def chunk(g):
                gs = ds(g, 1)
                chain[0] = 0
                split_lo(g, 0)
                split_lo(g, 1)
                split_lo(g, 2)
                split_lo(g, 3)
                dve.wait_ge(vst, 16 * g)
                for q in range(QT):
                    dve.wait_ge(vturn, QT * g + q + 1)
                    if q < z.NQ:
                        nc.vector.tensor_copy(W[3][:, 512 * q:512 * q + 512], px[q % 2][:]).then_inc(vcopy, 1)
                    else:
                        nc.vector.tensor_copy(vs[:], px[q % 2][0:z.B, 0:P]).then_inc(vcopy, 1)
                dve.wait_ge(vstd, 2 * g + 2)
                then(g, nc.vector.reciprocal(ss[:, 0:z.NT, 2], ss[:, 0:z.NT, 1]), CH)
                then(g, nc.vector.reciprocal(ss[0:z.B, z.NT, 2:3], ss[0:z.B, z.NT, 1:2]), CH)
                dve.wait_ge(vcopy, QT * g + QT)
                v3 = W[3][:, 0:T].rearrange("p (n d) -> p n d", d=P)
                then(g, nc.vector.tensor_tensor(v3, v3, ss[:, 0:z.NT, 2:3].broadcast_to([P, z.NT, P]), ALU.mult), CH)
                nc.vector.tensor_tensor(v3, v3, C.gv[:].rearrange("p (g d) -> p g d", d=P)[:, gs, :].broadcast_to([P, z.NT, P]),
                                        ALU.mult).then_inc(vready, 1)
                nc.vector.scalar_tensor_tensor(out=vs[:], in0=vs[:], scalar=ss[0:z.B, z.NT, 2:3],
                                               in1=C.gv[0:z.B].rearrange("p (g d) -> p g d", d=P)[:, gs, :].rearrange("p o d -> p (o d)"),
                                               op0=ALU.mult, op1=ALU.mult).then_inc(vready, 1)
                dve.wait_ge(evac, (TILES * g + 3) * NCH)
                then(g, nc.vector.tensor_tensor(W[1][:], W[1][:], W[2][:], ALU.mult), CH)
                split_lo(g, 4)
                bsv = C.bs[:].rearrange("p (g d) -> p g d", d=P)
                for q in range(QT):
                    dve.wait_ge(sturn, QT * g + q + 1)
                    if q < z.NQ:
                        t3 = tmp[:].rearrange("p (n d) -> p n d", d=P)
                        nc.vector.tensor_tensor(t3, px[2 - q % 2][:].rearrange("p (n d) -> p n d", d=P),
                                                bsv[:, gs, :].broadcast_to([P, 4, P]), ALU.add).then_inc(sread, 1)
                        w, src = 512, tmp[:]
                    else:
                        nc.vector.tensor_tensor(tmp[:, 0:z.B], px[2 - q % 2][:, 0:z.B],
                                                bsv[:, gs, 0:1].rearrange("p o d -> p (o d)").broadcast_to([P, z.B]),
                                                ALU.add).then_inc(sread, 1)
                        w, src = z.B, tmp[:, 0:z.B]
                    dve.wait_ge(sread, QT * g + q + 1)
                    ins = nc.vector.tensor_tensor(W[1][:, 512 * q:512 * q + w], W[1][:, 512 * q:512 * q + w], src, ALU.mult)
                    ins.then_inc(amix, 1)
                    dve.wait_ge(amix, QT * g + q + 1)
                nc.vector.memset(W[3][:, 0:z.TAPS - 1], 0.0).then_inc(zeroed, 1)
                K = z.TAPS - 1
                dve.wait_ge(evac, (TILES * g + 4) * NCH)
                cw = lambda k: C.convw[:, gs, k:k + 1].rearrange("p o k -> p (o k)")
                cb = C.convb[:, gs]
                then(g, nc.vector.tensor_scalar(W[4][:, 0:T], W[3][:, 0:T], cw(0), cb, ALU.mult, ALU.add), CH)
                for k in range(1, z.TAPS):
                    then(g, nc.vector.scalar_tensor_tensor(out=W[4][:, 0:T], in0=W[3][:, k:k + T], scalar=cw(k), in1=W[4][:, 0:T],
                                                           op0=ALU.mult, op1=ALU.add), CH)
                then(g, nc.vector.tensor_scalar(W[4][:, T:TP], W[3][:, T + K:TP + K], cw(K), cb, ALU.mult, ALU.add), CH)
                for k in range(K):
                    stc = C.stc[:].rearrange("p g (b k) -> p g b k", k=K)[:, gs, :, k:k + 1].rearrange("p o b k -> p (o b k)")
                    ins = nc.vector.scalar_tensor_tensor(out=W[4][:, T:TS], in0=stc, scalar=cw(k), in1=W[4][:, T:TS],
                                                         op0=ALU.mult, op1=ALU.add)
                    if k < K - 1:
                        then(g, ins, CH)
                    else:
                        ins.then_inc(xcready, 1)
                nc.vector.tensor_copy(keep[:, 0, gs, :].rearrange("p o n -> p (o n)"), W[3][:, T:T + K + z.B]).then_inc(kept, 1)
                dve.wait_ge(gated, 2 * NCH * g + 2 * NCH)
                then(g, nc.vector.tensor_tensor(W[2][:], W[2][:], W[4][:], ALU.mult), CH)
                dve.wait_ge(aexp, g + 1)
                then(g, nc.vector.tensor_tensor(W[4][:], W[3][:, 0:TP], W[3][:, 0:TP], ALU.mult), CH)
                dve.wait_ge(th, g + 1)
                nc.vector.scalar_tensor_tensor(out=W[4][:], in0=W[4][:], scalar=1.0, in1=W[0][:], op0=ALU.add,
                                               op1=ALU.mult).then_inc(bpre, 1)
                dve.wait_ge(bsq, g + 1)
                then(g, nc.vector.tensor_tensor(W[4][:], W[4][:], W[2][:], ALU.mult), CH)
                nc.vector.tensor_tensor_scan(W[0][:, 0:T], W[3][:, 0:T], W[4][:, 0:T], 0.0, ALU.mult, ALU.add).then_inc(conv, 1)
                h0 = C.h0[:, gs, :].rearrange("p o b -> p (o b)")
                then(g, nc.vector.tensor_tensor(W[0][:, T:TS], W[3][:, T:TS], h0, ALU.mult), CH)
                then(g, nc.vector.tensor_tensor(W[0][:, T:TS], W[0][:, T:TS], W[4][:, T:TS], ALU.add), CH)
                dve.wait_ge(conv, g + 1)
                nc.vector.tensor_copy(keep[:, 1, gs, :].rearrange("p o n -> p (o n)"), W[0][:, T - K:T + z.B]).then_inc(kept, 1)
                nc.vector.tensor_tensor(W[1][:, 0:TS], W[1][:, 0:TS], W[0][:, 0:TS], ALU.mult).then_inc(bready, 1)
                assert chain[0] == CH, chain[0]

            each(dve, z.G, chunk)
            for x in range(2):
                dve.wait_ge(kturn, x + 1)
                nc.vector.tensor_copy(rows[:, x, :], px[x][0:z.TAPS - 1 + z.B, 0:z.AW]).then_inc(kcopy, 1)


def project1(nc, z, a, C, xh, xl, D, out):
    T, TS, TP, CW, NCH, B = z.T, z.TS, z.TP, z.CW, z.NCH, z.B
    QT = z.NQ + 1
    with ExitStack() as ctx:
        S = Stage(nc, ctx, "p1")
        raw = S.sb("raw", [P, z.KB, P])
        wh = S.sb("wh", [P, 2, z.KB, P], F32R)
        wl = S.sb("wl", [P, 2, z.KB, P], F32R)
        A = S.sb("a", [P, TP])
        Bk = S.sb("b", [P, TP])
        R = [S.sb(f"r{x}", [P, TP]) for x in range(2)]
        Hh = S.sb("h", [P, TP])
        rows = S.sb("rows", [P, 2, 4, P])
        srow = S.sb("srow", [B, 3, P])
        pb = [S.ps(f"pb{c}", [P, 512]) for c in range(NCH)]
        px = [S.ps(f"px{c}", [P, 512]) for c in range(3)]
        (raw_in, hi, lo, proj, evac, ssum, rooted, recd, dv, normed, hidone, lodone, hst, lst, gst, turn, rcopy, sqd, rst0, rst1, srst,
         fact, fdve, fturn, fcopy, fst, padw) = S.sems(
            "raw_in hi lo projected evacuated sumsq rooted recd dv normed hidone lodone hi_stored lo_stored g_stored turned"
            " rows_copied squared rows_stored0 rows_stored1 srows_stored fact fdve fturned fcopied fstored padw")
        rst = (rst0, rst1)
        cols = [0, z.D, 2 * z.D, 3 * z.D]
        block = ctx.enter_context(nc.Block())

        NTURN = 1 + 2 * QT

        @block.sync
        def _(sp):
            def pair(p):
                for j in range(4):
                    sp.wait_ge(lo, 4 * p + j)
                    sp.dma_start(raw[:], a["w_in1"][:, ds(cols[j] + P * p, P)].rearrange("(k p) n -> p k n", p=P)).then_inc(raw_in, 16)

            each(sp, z.PAIRS, pair)
            sp.wait_ge(padw, 1)
            sp.dma_start(raw[:, :, 0:z.H], a["w_in1"][:, 4 * z.D:4 * z.D + z.H].rearrange("(k p) n -> p k n", p=P)).then_inc(raw_in, 16)

        @block.gpsimd
        def _(pool):
            def store_rows(p, x, name, turn0):
                for q in range(z.NQ):
                    s = (x * z.NQ + q) % 2
                    wait_apart(pool, rcopy, NTURN * p + turn0 + q + 1, raw_in, 16)
                    pool.dma_start(out[name + "_prompt"][0, 512 * q:512 * q + 512, ds(2 * p, 2), :].rearrange("(t r) h d -> r t (h d)", r=P),
                                   rows[:, s]).then_inc(rst[s], 16)

            def pair(p):
                fs = ds(P * p, P)
                wait_apart(pool, hidone, 2 * p + 1, raw_in, 16)
                pool.dma_start(D.qh[fs, :], Hh[:, 0:T]).then_inc(hst, 16)
                wait_apart(pool, lodone, 2 * p + 1, raw_in, 16)
                pool.dma_start(D.ql[fs, :], R[0][:, 0:T]).then_inc(lst, 16)
                store_rows(p, 0, "k", 1)
                wait_apart(pool, evac, (4 * p + 4) * NCH, raw_in, 16)
                pool.dma_start(D.sg[fs, :], R[0][:, 0:TS]).then_inc(gst, 16)
                wait_apart(pool, hidone, 2 * p + 2, raw_in, 16)
                pool.dma_start(D.kh[fs, :], Hh[:, 0:T]).then_inc(hst, 16)
                wait_apart(pool, lodone, 2 * p + 2, raw_in, 16)
                pool.dma_start(D.kl[fs, :], R[1][:, 0:T]).then_inc(lst, 16)
                store_rows(p, 1, "v", 1 + QT)
                wait_apart(pool, rcopy, NTURN * p + NTURN, raw_in, 16)
                pool.dma_start(D.qs[:, fs], srow[:, 0]).then_inc(srst, 16)
                pool.dma_start(out["k_sample"][:, 0, ds(2 * p, 2), :].rearrange("b h d -> b (h d)"), srow[:, 1]).then_inc(srst, 16)
                pool.dma_start(out["v_sample"][:, 0, ds(2 * p, 2), :].rearrange("b h d -> b (h d)"), srow[:, 2]).then_inc(srst, 16)

            each(pool, z.PAIRS, pair)
            pool.wait_ge(fdve, 4)
            pool.dma_start(D.nck[:], R[1][0:z.H, 0:T]).then_inc(fst, 16)
            pool.wait_ge(fcopy, 3)
            pool.dma_start(out["logf_prompt"][0].rearrange("(t r) h -> r t h", r=P),
                           rows[:, 0].rearrange("p t n -> p (t n)")[:, 0:z.NT * z.H].rearrange("p (t h) -> p t h", h=z.H)).then_inc(fst, 16)
            pool.dma_start(out["logf_sample"][:, 0, :], srow[:, 0, 0:z.H]).then_inc(fst, 16)
            pool.wait_ge(fst, 48)
            for sm, n in ((hst, 32 * z.PAIRS), (lst, 32 * z.PAIRS), (gst, 16 * z.PAIRS), (srst, 48 * z.PAIRS),
                          (rst0, 16 * z.NQ * z.PAIRS), (rst1, 16 * z.NQ * z.PAIRS)):
                pool.wait_ge(sm, n)

        @block.tensor
        def _(pe):
            def project(p, j):
                s = j % 2
                pe.wait_ge(lo, 4 * p + j + 1)
                for c in range(NCH):
                    pe.wait_ge(evac, 4 * NCH * p if j == 0 else (4 * p + j - 1) * NCH + c + 1)
                    for k in range(z.KB):
                        last = split3(nc, pb[c][:, 0:CW], (wh[:, s, k, :], wl[:, s, k, :]),
                                      (xh[:, k, c * CW:(c + 1) * CW], xl[:, k, c * CW:(c + 1) * CW]), k, z.KB)
                    last.then_inc(proj, 1)

            def sums(p, x):
                pe.wait_ge(sqd, 2 * NCH * p + (x + 1) * NCH)
                pe.wait_ge(rooted, 2 * NCH * p + x * NCH)
                pe.wait_ge(rcopy, NTURN * p + x)
                for c in range(NCH):
                    if c >= 3:
                        pe.wait_ge(rooted, 2 * NCH * p + x * NCH + c - 2)
                    nc.tensor.matmul(px[c % 3][:, 0:CW], C.pairsum[:], R[x][:, c * CW:(c + 1) * CW], start=True, stop=True).then_inc(ssum, 1)

            def turns(p, src, turn0):
                for q in range(QT):
                    m = turn0 + q
                    pe.wait_ge(rcopy, NTURN * p + m - 1)
                    for t in range(4 if q < z.NQ else 1):
                        n = P if q < z.NQ else B
                        col = (4 * q + t) * P
                        last = nc.tensor.transpose(px[1 + m % 2][0:n, t * P:(t + 1) * P], src[:, col:col + n], C.ident[:])
                    last.then_inc(turn, 1)

            def pair(p):
                project(p, 0)
                project(p, 1)
                sums(p, 0)
                project(p, 2)
                pe.wait_ge(normed, 2 * p + 1)
                nc.tensor.transpose(px[1][0:B, 0:P], A[:, T:TS], C.ident[:]).then_inc(turn, 1)
                sums(p, 1)
                project(p, 3)
                pe.wait_ge(normed, 2 * p + 2)
                turns(p, Bk, 1)
                pe.wait_ge(evac, (4 * p + 3) * NCH)
                turns(p, A, 1 + QT)

            each(pe, z.PAIRS, pair)
            project(z.PAIRS, 0)
            pe.wait_ge(fdve, 3)
            for x in range(2):
                for t in range(z.NT):
                    last = nc.tensor.transpose(px[x][:, t * z.H:(t + 1) * z.H], (A if x == 0 else Bk)[0:z.H, t * P:(t + 1) * P],
                                               C.ident[0:z.H, 0:z.H])
                last.then_inc(fturn, 1)
            nc.tensor.transpose(px[2][0:B, 0:z.H], A[0:z.H, T:TS], C.ident[0:z.H, 0:z.H]).then_inc(fturn, 1)

        @block.scalar
        def _(act):
            def split_hi(p, j):
                act.wait_ge(raw_in, 16 * (4 * p + j + 1))
                act.wait_ge(proj, 4 * NCH * p if j < 2 else (4 * p + j - 1) * NCH)
                nc.scalar.activation(wh[:, j % 2], raw[:], ACT.Copy).then_inc(hi, 1)

            def evacuate(p, j, dst, func, squares=None):
                for c in range(NCH):
                    cs = slice(c * CW, (c + 1) * CW)
                    act.wait_ge(proj, (4 * p + j) * NCH + c + 1)
                    if squares is not None:
                        nc.scalar.activation(squares[:, cs], pb[c][:, 0:CW], ACT.Square).then_inc(sqd, 1)
                        act.wait_ge(sqd, (2 * p + j) * NCH + c + 1)
                    nc.scalar.activation(dst[:, cs], pb[c][:, 0:CW], func).then_inc(evac, 1)

            def root(p, x):
                for c in range(NCH):
                    act.wait_ge(ssum, 2 * NCH * p + x * NCH + c + 1)
                    nc.scalar.activation(R[x][:, c * CW:(c + 1) * CW], px[c % 3][:, 0:CW], ACT.Sqrt, scale=1.0 / z.HD,
                                         bias=C.eps[:]).then_inc(rooted, 1)

            def pair(p):
                split_hi(p, 0)
                split_hi(p, 1)
                act.wait_ge(rcopy, NTURN * p)
                act.wait_ge(gst, 16 * p)
                evacuate(p, 0, A, ACT.Copy, R[0])
                split_hi(p, 2)
                act.wait_ge(lst, 32 * p)
                evacuate(p, 1, Bk, ACT.Copy, R[1])
                split_hi(p, 3)
                root(p, 0)
                act.wait_ge(normed, 2 * p + 1)
                act.wait_ge(hst, 32 * p)
                nc.scalar.activation(Hh[:].bitcast(F32R), A[:], ACT.Copy).then_inc(hidone, 1)
                act.wait_ge(lodone, 2 * p + 1)
                act.wait_ge(rcopy, NTURN * p + 1)
                act.wait_ge(hidone, 2 * p + 1)
                evacuate(p, 2, A, ACT.Copy)
                root(p, 1)
                act.wait_ge(lst, 32 * p + 16)
                evacuate(p, 3, R[0], ACT.Silu)
                act.wait_ge(normed, 2 * p + 2)
                act.wait_ge(hst, 32 * p + 16)
                nc.scalar.activation(Hh[:].bitcast(F32R), Bk[:], ACT.Copy).then_inc(hidone, 1)

            each(act, z.PAIRS, pair)
            N = z.PAIRS
            split_hi(N, 0)
            act.wait_ge(rcopy, NTURN * N)
            act.wait_ge(hst, 32 * N)
            for c in range(NCH):
                act.wait_ge(proj, 4 * N * NCH + c + 1)
                nc.scalar.activation(A[0:z.H, c * CW:(c + 1) * CW], pb[c][0:z.H, 0:CW], ACT.Identity, bias=C.bf[:]).then_inc(fact, 1)
            act.wait_ge(fact, NCH)
            nc.scalar.activation(Hh[0:z.H], A[0:z.H], ACT.Abs).then_inc(fact, 1)
            act.wait_ge(fact, NCH + 1)
            nc.scalar.activation(Hh[0:z.H], Hh[0:z.H], ACT.Exp, scale=-1.0).then_inc(fact, 1)
            act.wait_ge(fact, NCH + 2)
            nc.scalar.activation(Hh[0:z.H], Hh[0:z.H], ACT.Ln, bias=1.0).then_inc(fact, 1)

        @block.vector
        def _(dve):
            def split_lo(p, j):
                dve.wait_ge(hi, 4 * p + j + 1)
                nc.vector.tensor_tensor(wl[:, j % 2], raw[:], wh[:, j % 2].bitcast(F32), ALU.subtract).then_inc(lo, 1)

            def normalise(p, x, t, g):
                dve.wait_ge(rooted, 2 * NCH * p + (x + 1) * NCH)
                nc.vector.reciprocal(R[x][:], R[x][:]).then_inc(recd, 1)
                dve.wait_ge(recd, 2 * p + x + 1)
                dve.wait_ge(evac, (4 * p + x + 1) * NCH)
                nc.vector.scalar_tensor_tensor(out=t[:], in0=t[:], scalar=g[:], in1=R[x][:], op0=ALU.mult,
                                               op1=ALU.mult).then_inc(normed, 1)

            def low_part(p, x, t):
                dve.wait_ge(hidone, 2 * p + x + 1)
                dve.wait_ge(normed, 2 * p + x + 1)
                nc.vector.tensor_tensor(R[x][:].bitcast(F32R), t[:], Hh[:], ALU.subtract).then_inc(lodone, 1)

            def copy_rows(p, x, turn0):
                for q in range(QT):
                    m = turn0 + q
                    dve.wait_ge(turn, NTURN * p + m + 1)
                    if q < z.NQ:
                        n = x * z.NQ + q
                        dve.wait_ge(rst[n % 2], 16 * (z.NQ * p + n // 2))
                        nc.vector.tensor_copy(rows[:, n % 2].rearrange("p t n -> p (t n)"), px[1 + m % 2][:]).then_inc(rcopy, 1)
                    else:
                        nc.vector.tensor_copy(srow[:, 1 + x], px[1 + m % 2][0:B, 0:P]).then_inc(rcopy, 1)

            def pair(p):
                for j in range(4):
                    split_lo(p, j)
                normalise(p, 0, A, C.qg)
                low_part(p, 0, A)
                dve.wait_ge(turn, NTURN * p + 1)
                dve.wait_ge(srst, 48 * p)
                nc.vector.tensor_copy(srow[:, 0], px[1][0:B, 0:P]).then_inc(rcopy, 1)
                normalise(p, 1, Bk, C.kg)
                copy_rows(p, 0, 1)
                low_part(p, 1, Bk)
                copy_rows(p, 1, 1 + QT)

            each(dve, z.PAIRS, pair)
            N = z.PAIRS
            dve.wait_ge(lo, 4 * N)
            nc.vector.memset(raw[:, :, z.H:P], 0.0).then_inc(padw, 1)
            dve.wait_ge(padw, 1)
            split_lo(N, 0)
            dve.wait_ge(gst, 16 * N)
            nc.vector.memset(R[0][0:z.H, 0:T], 1.0).then_inc(fdve, 1)
            dve.wait_ge(fact, NCH + 3)
            nc.vector.scalar_tensor_tensor(out=A[0:z.H], in0=A[0:z.H], scalar=0.0, in1=Hh[0:z.H], op0=ALU.min,
                                           op1=ALU.subtract).then_inc(fdve, 1)
            dve.wait_ge(fdve, 2)
            dve.wait_ge(lst, 32 * N)
            nc.vector.tensor_tensor_scan(Bk[0:z.H, 0:T], R[0][0:z.H, 0:T], A[0:z.H, 0:T], 0.0, ALU.mult, ALU.add).then_inc(fdve, 1)
            dve.wait_ge(fdve, 3)
            nc.vector.tensor_scalar(R[1][0:z.H, 0:T].bitcast(F32R), Bk[0:z.H, 0:T], -1.0, None, ALU.mult).then_inc(fdve, 1)
            dve.wait_ge(fturn, 3)
            dve.wait_ge(rst0, 16 * z.NQ * N)
            dve.wait_ge(srst, 48 * N)
            nc.vector.tensor_copy(rows[:, 0].rearrange("p t n -> p (t n)")[:, 0:z.NT * z.H], px[0][:, 0:z.NT * z.H]).then_inc(fcopy, 1)
            nc.vector.tensor_scalar(C.nckt[:].rearrange("p t h -> p (t h)"), px[1][:, 0:z.NT * z.H], -1.0, None, ALU.mult).then_inc(fcopy, 1)
            nc.vector.tensor_copy(srow[:, 0, 0:z.H], px[2][0:B, 0:z.H]).then_inc(fcopy, 1)
            dve.wait_ge(fcopy, 3)


def past(nc, z, a, C, out):
    with ExitStack() as ctx:
        S = Stage(nc, ctx, "pa")
        NG = z.B // z.SB
        idx = S.sb("idx", [z.GP, NG], I32)
        L = S.sb("l", [z.GP, NG, P * z.H])
        cum = S.sb("cum", [z.GP, NG, z.H, P])
        ones = S.sb("ones", [z.GP, P])
        tot = S.sb("tot", [z.GP, NG, z.H])
        later = S.sb("later", [z.GP, z.GP])
        lnew = S.sb("lnew", [1, z.B * z.H])
        pl = S.ps("pl", [P, 512])
        pt = [S.ps(f"pt{x}", [P, 512]) for x in range(2)]
        idx_in, l_in, new_in, made, totd, latm, dv, turned, copied, scand = S.sems("idx_in l_in new_in made tot later dv turned copied scanned")
        block = ctx.enter_context(nc.Block())

        @block.sync
        def _(sp):
            for n in range(NG):
                sp.dma_start(idx[:, n:n + 1], a["page_table"][n * z.SB:(n + 1) * z.SB, :].rearrange("b g -> (b g)")
                             .rearrange("(q o) -> q o", o=1)).then_inc(idx_in, 16)
            sp.dma_start(lnew[:], out["logf_sample"].rearrange("b o h -> o (b h)")).then_inc(new_in, 16)

        @block.gpsimd
        def _(pool):
            nc.gpsimd.memset(ones[:], 1.0).then_inc(made, 1)
            nc.gpsimd.memset(later[:], 1.0).then_inc(made, 1)
            nc.gpsimd.memset(C.decay[:, :, :, z.PG:z.PX], NEG).then_inc(made, 1)
            pool.wait_ge(made, 3)
            nc.gpsimd.affine_select(out=later[:], in_=later[:], compare_op=ALU.is_gt, fill=0.0, base=0,
                                    pattern=[[-1, z.GP]], channel_multiplier=1).then_inc(made, 1)
            pool.wait_ge(made, 4)
            lv = later[:].rearrange("q (b g) -> q b g", g=z.PG)
            nc.gpsimd.affine_select(out=lv, in_=lv, compare_op=ALU.is_ge, fill=0.0, base=z.PG - 1,
                                    pattern=[[z.PG, z.SB], [0, z.PG]], channel_multiplier=-1).then_inc(made, 1)
            pool.wait_ge(idx_in, 16 * NG)
            for n in range(NG):
                pool.indirect_dma_start(out=L[:, n, :], out_offset=None, in_=a["cache_logf"].rearrange("n p h -> n (p h)"),
                                        in_offset=bass.IndirectOffsetOnAxis(ap=idx[:, n:n + 1].bitcast(U32), axis=0)).then_inc(l_in, 16)
            pool.wait_ge(l_in, 16 * NG)

        @block.tensor
        def _(pe):
            pe.wait_ge(made, 5)
            for n in range(NG):
                pe.wait_ge(totd, n + 1)
                nc.tensor.matmul(pl[0:z.GP, n * z.H:(n + 1) * z.H], later[:], tot[:, n, :], start=True, stop=True).then_inc(latm, 1)
            m = 0
            for n in range(NG):
                pe.wait_ge(dv, 3 * n + 3)
                for h4 in range(0, z.H, 4):
                    if m >= 2:
                        pe.wait_ge(copied, m - 1)
                    for h in range(4):
                        last = nc.tensor.transpose(pt[m % 2][:, h * z.GP:(h + 1) * z.GP], cum[:, n, h4 + h, :], C.ident[0:z.GP, 0:z.GP])
                    last.then_inc(turned, 1)
                    m += 1

        @block.vector
        def _(dve):
            dve.wait_ge(made, 1)
            dve.wait_ge(l_in, 16 * NG)
            for n in range(NG):
                lv = L[:, n, :].rearrange("q (t h) -> q t h", h=z.H)
                for h in range(z.H):
                    last = nc.vector.tensor_tensor_scan(cum[:, n, h, :], ones[:], lv[:, :, h], 0.0, ALU.mult, ALU.add)
                last.then_inc(scand, 1)
                dve.wait_ge(scand, n + 1)
                nc.vector.tensor_copy(tot[:, n, :], cum[:, n, :, P - 1]).then_inc(totd, 1)
            for n in range(NG):
                dve.wait_ge(latm, NG)
                dve.wait_ge(totd, n + 1)
                nc.vector.tensor_tensor(tot[:, n, :], tot[:, n, :], pl[0:z.GP, n * z.H:(n + 1) * z.H], ALU.add).then_inc(dv, 1)
                dve.wait_ge(dv, 3 * n + 1)
                nc.vector.tensor_scalar(cum[:, n], cum[:, n], -1.0, None, ALU.mult).then_inc(dv, 1)
                dve.wait_ge(dv, 3 * n + 2)
                nc.vector.tensor_tensor(cum[:, n], cum[:, n], tot[:, n, :].rearrange("q (h o) -> q h o", o=1).broadcast_to([z.GP, z.H, P]),
                                        ALU.add).then_inc(dv, 1)
            m = 0
            for n in range(NG):
                for h4 in range(0, z.H, 4):
                    dve.wait_ge(turned, m + 1)
                    nc.vector.tensor_copy(C.decay[:, n * z.SB:(n + 1) * z.SB, h4:h4 + 4, 0:z.PG].rearrange("p b h g -> p h b g"),
                                          pt[m % 2][:, 0:4 * z.GP].rearrange("p (h b g) -> p h b g", h=4, g=z.PG)).then_inc(copied, 1)
                    m += 1
            dve.wait_ge(new_in, 16)
            dve.wait_ge(made, 3)
            nc.vector.tensor_scalar(C.decay[0:1, :, :, z.PG:z.PX].rearrange("p b h o -> p (b h o)"), lnew[:], -1.0, None,
                                    ALU.mult).then_inc(copied, 1)
            dve.wait_ge(copied, m + 1)


def attention(nc, z, a, C, D, out):
    T, TS, B, H, HD, PG, PX = z.T, z.TS, z.B, z.H, z.HD, z.PG, z.PX
    NC = T // 512
    HR = HD + 1
    NS = 2 * sum(4 * (c + 1) for c in range(NC))
    VI = PG // 4 + 1
    with ExitStack() as ctx:
        S = Stage(nc, ctx, "at")
        Q1 = [S.sb(f"q1_{s}", [P, T], F32R) for s in range(2)]
        Q2 = [S.sb(f"q2_{s}", [HR, T], F32R) for s in range(2)]
        K1 = [S.sb(f"k1_{s}", [P, T], F32R) for s in range(2)]
        K2 = [S.sb(f"k2_{s}", [HR, T], F32R) for s in range(2)]
        KM = [S.sb(f"km_{s}", [HR, T], F32R) for s in range(2)]
        V = [S.sb(f"v_{s}", [P, z.NT, HR]) for s in range(2)]
        SG = [S.sb(f"sg_{s}", [HD, T]) for s in range(2)]
        W = [S.sb(f"w_{x}", [P, 512]) for x in range(3)]
        og = [S.sb(f"og_{x}", [HR, 512]) for x in range(2)]
        mx = S.sb("mx", [P, 2, 4, NC])
        mneg = S.sb("mneg", [P, 2, 4])
        maskf = S.sb("maskf", [P, P])
        maskr = S.sb("maskr", [P, P], F32R)
        identr = S.sb("identr", [P, P], F32R)
        pt = S.sb("pt", [1, B * PG], I32)
        kp = S.sb("kp", [P, 4, z.D])
        vp = S.sb("vp", [P, 4, z.D])
        knew = S.sb("knew", [P, z.D])
        vnew = S.sb("vnew", [P, z.D])
        qb = S.sb("qb", [P, z.D])
        prod = S.sb("prod", [P, z.D])
        sc = S.sb("sc", [P, H, PX])
        sd = S.sb("sd", [P, H, PX])
        sw = S.sb("sw", [P, PX, 32])
        smx = S.sb("smx", [P, H])
        smh = S.sb("smh", [H, 1])
        smd = S.sb("smd", [H, H])
        onesh = S.sb("onesh", [H, P])
        l4 = S.sb("l4", [P, 4, 32])
        rl = S.sb("rl", [P, 2])
        headmask = S.sb("headmask", [P, z.D])
        cm = S.sb("cm", [P, z.D])
        atts = S.sb("atts", [P, z.KB, B])
        sgs = S.sb("sgs", [P, z.KB, B])
        ones = S.sb("ones", [H, B])
        MX = [S.ps(f"mx{x}", [P, 512]) for x in range(2)]
        ST = [S.ps(f"st{x}", [P, 512]) for x in range(2)]
        O = S.ps("o", [P, 512])
        MR = S.ps("mr", [1, 512])
        CV = S.ps("cv", [P, 2, 512])
        (mdone, mread, mnd, mrd, rowd, qk, ex, pv, oed, oea, onesd, pt_in, knew_in, vnew_in, qb_in, kmul, kred, sdd,
         smaxd, sall, ssub, sexp, ssum, sl4, slmm, srcp, vdone, vmask, vatt, vcopy, made, masked, sgs_in, fin, fst, sl1, rlw, dvm, sdiag, sspread, smhd) = S.sems(
            "max_product max_read max_neg max_turned max_row scores weights summed left_dve left_act ones_set table_in knew_in vnew_in"
            " qb_in k_times_q k_reduced decayed smax sall ssub sexp ssum sl4 slsum srcp vpages vmasked vatt vcopied made masked sgs_in final fstored sl1 rl_bounded masks_rounded sdiag sspread smhd")
        ld = S.sems("head_in0 head_in1")
        ogst = S.sems("out_stored0 out_stored1")
        k_in = S.sems("k_in0 k_in1 k_in2 k_in3")
        v_in = S.sems("v_in0 v_in1 v_in2 v_in3")
        NLD = 10

        def schedule(keys, values, last):
            segs = [[(u, j, seg) for j in range(4) for seg in range(u % NC + 1)] for u in range(2 * NC)]
            side_k = [w for g in range(PX) for w in (("KM", g), ("KR", g))] + [("SD",)] if keys else []
            side_v = ([("SM",), ("SA",), ("SB",), ("SC",), ("SS",), ("SE",), ("SL",), ("SX",), ("SR",)] + [("VG", r) for r in range(PG // 4)]
                      + [("VN",), ("VM",), ("VA",), ("VC",)]) if values else []
            seq, m, n = [], 0, 0
            for s in segs[0]:
                seq.append(("M", *s, m))
                m += 1
            seq += [("MN", 0), ("MR", 0)]
            pending = None
            for u in range(2 * NC):
                c = u % NC
                nxt = segs[u + 1] if u + 1 < 2 * NC else []
                steps, at = 4 * (c + 1), 0
                for kb in range(steps):
                    if pending and kb == 0:
                        seq += [("PV", *pending), ("OE", pending[0])]
                    if kb == 0 and c == 0 and not (last and u // NC == 1):
                        seq.append(("LD", u // NC))
                    seq.append(("QK", u, kb, n))
                    if kb == steps - 1 and nxt:
                        seq.append(("MR", u + 1))
                    upto = len(nxt) if kb >= steps - 2 else -(-len(nxt) * (kb + 1) // (steps - 1))
                    new = nxt[at:upto]
                    at = upto
                    for s in new:
                        seq.append(("M", *s, m))
                        m += 1
                    if new and at == len(nxt):
                        seq.append(("MN", u + 1))
                    if kb:
                        seq.append(("PV", *pending))
                    pending = (u, kb, n)
                    n += 1
                    for side in (side_k, side_v):
                        a0, a1 = (len(side) * (n - 1)) // NS, (len(side) * n) // NS
                        seq += side[a0:a1]
            seq += [("PV", *pending), ("OE", pending[0])]
            assert m == n == NS
            return seq

        block = ctx.enter_context(nc.Block())

        def iterations(eng, body):
            body(0, schedule(True, False, False), True)
            if B > 2:
                with eng.Fori(1, B - 1) as i:
                    body(i, schedule(True, True, False), False)
            body(B - 1, schedule(True, True, True), False)

        tail = [("SM",), ("SA",), ("SB",), ("SC",), ("SS",), ("SE",), ("SL",), ("SX",), ("SR",)] + [("VG", r) for r in range(PG // 4)] \
            + [("VN",), ("VM",), ("VA",), ("VC",)]

        @block.sync
        def _(sp):
            def page(dst, cache, n):
                r = sp.value_load(pt[0:1, ds(n, 1)], min_val=0, max_val=z.POOL - 1)
                return sp.dma_start(dst, cache[ds(r, 1)].rearrange("o p h d -> p (o h d)"))

            def head(h, s):
                hs = ds(HD * h, HD)
                for dst, src in ((Q1[s][0:HD], D.qh[hs, :]), (Q1[s][HD:P], D.ql[hs, :]), (Q2[s][0:HD], D.qh[hs, :]),
                                 (K1[s][0:HD], D.kh[hs, :]), (K1[s][HD:P], D.kh[hs, :]), (K2[s][0:HD], D.kl[hs, :]),
                                 (KM[s][0:HD], D.kh[hs, :]), (KM[s][HD:HR], D.nck[ds(h, 1), :]),
                                 (SG[s][:], D.sg[hs, 0:T]),
                                 (V[s][:, :, 0:HD], out["v_prompt"][0, :, ds(h, 1), :].rearrange("(t r) o d -> r t (o d)", r=P))):
                    sp.dma_start(dst.bitcast(F32), src).then_inc(ld[s], 16)

            def sample_rows(b, free=None):
                sp.dma_start(knew[0:1, :], out["k_sample"][ds(b, 1)].rearrange("o t h d -> (o t) (h d)")).then_inc(knew_in, 16)
                sp.dma_start(qb[:], D.qs[ds(b, 1), :].rearrange("o d -> (o d)").partition_broadcast(P)).then_inc(qb_in, 16)

            def run(i, seq, first, last):
                for w in seq:
                    if w[0] == "LD":
                        s = w[1]
                        if s == 0:
                            if not first:
                                wait_apart(sp, oed, 2 * NC * i, pt_in, 16)
                            head(2 * i + 1, 1)
                        else:
                            wait_apart(sp, oed, 2 * NC * i + NC, pt_in, 16)
                            head(2 * i + 2, 0)
                    elif w[0] == "KM":
                        g = w[1]
                        if last and g >= PG - 4:
                            continue
                        wait_apart(sp, kmul, PX * i + g + 1, pt_in, 16)
                        if g < PG:
                            page(kp[:, g % 4], a["cache_k"], PG * i + g + 4).then_inc(k_in[g % 4], 16)
                        else:
                            sample_rows(i + 1)
                    elif w[0] == "VG":
                        values(i - 1, w[1], False)
                    elif w[0] == "VN":
                        sp.wait_ge(vdone, VI * (i - 1) + VI)
                        sp.dma_start(vnew[0:1, :], out["v_sample"][ds(i, 1)].rearrange("o t h d -> (o t) (h d)")).then_inc(vnew_in, 16)

            def values(b, r, end):
                if end and r == PG // 4 - 1:
                    return
                wait_apart(sp, vdone, VI * b + r + 1, pt_in, 16)
                for g in range(4):
                    page(vp[:, g], a["cache_v"], PG * b + 4 * r + 4 + g).then_inc(v_in[g], 16)

            sp.dma_start(pt[:], a["page_table"].rearrange("b g -> (b g)").rearrange("(o n) -> o n", o=1)).then_inc(pt_in, 16)
            head(0, 0)
            sp.wait_ge(pt_in, 16)
            sp.wait_ge(made, 3)
            sample_rows(0)
            sp.dma_start(vnew[0:1, :], out["v_sample"][0:1].rearrange("o t h d -> (o t) (h d)")).then_inc(vnew_in, 16)
            for g in range(4):
                page(kp[:, g], a["cache_k"], g).then_inc(k_in[g], 16)
            for g in range(4):
                page(vp[:, g], a["cache_v"], g).then_inc(v_in[g], 16)
            run(0, schedule(True, False, False), True, False)
            if B > 2:
                with sp.Fori(1, B - 1) as i:
                    run(i, schedule(True, True, False), False, False)
            run(B - 1, schedule(True, True, True), False, True)
            for r in range(PG // 4):
                values(B - 1, r, True)
            sp.dma_start(sgs[:], D.sg[:, T:TS].rearrange("(k p) b -> p k b", p=P)).then_inc(sgs_in, 16)
            sp.wait_ge(fin, 2)
            sp.dma_start(D.att[:, T:TS].rearrange("(k p) b -> p k b", p=P), atts[:]).then_inc(fst, 16)
            sp.dma_start(D.lsum[:, T:TS], ones[:]).then_inc(fst, 16)
            sp.wait_ge(fst, 32)

        @block.gpsimd
        def _(pool):
            for t in (knew, vnew, sw):
                nc.gpsimd.memset(t[:], 0.0).then_inc(made, 1)
            for s in range(2):
                nc.gpsimd.memset(V[s][:, :, HD:HR], 1.0).then_inc(made, 1)
            nc.gpsimd.memset(ones[:], 1.0).then_inc(made, 1)
            nc.gpsimd.memset(onesh[:], 1.0).then_inc(made, 1)
            nc.gpsimd.memset(headmask[:], 1.0).then_inc(masked, 1)
            nc.gpsimd.memset(maskf[:], 0.0).then_inc(masked, 1)
            pool.wait_ge(masked, 2)
            nc.gpsimd.affine_select(out=maskf[:], in_=maskf[:], compare_op=ALU.is_ge, fill=NEG, base=0,
                                    pattern=[[-1, P]], channel_multiplier=1).then_inc(masked, 1)
            for base, mult, off in ((0, 1, 0), (HD - 1, -1, 0)):
                for x in range(4):
                    pool.wait_ge(masked, (3 if mult == 1 else 7) + x)
                    hm = headmask[32 * x:32 * x + 32, :]
                    nc.gpsimd.affine_select(out=hm, in_=hm, compare_op=ALU.is_ge, fill=0.0, base=base,
                                            pattern=[[mult, z.D]], channel_multiplier=-mult * HD).then_inc(masked, 1)
            pool.wait_ge(masked, 11)
            for s in range(2):
                nc.gpsimd.memset(K2[s][HD:HR].bitcast(F32), 1.0).then_inc(made, 1)
                nc.gpsimd.memset(Q2[s][HD:HR].bitcast(F32), 1.0).then_inc(onesd, 1)
            pool.wait_ge(made, 9)
            pool.wait_ge(onesd, 2)

            def run(i, seq, first):
                for w in seq:
                    if w[0] == "OE":
                        u = w[1]
                        h, c, s = 2 * i + u // NC, u % NC, u % 2
                        wait_apart(pool, oed, 2 * NC * i + u + 1, made, 9)
                        pool.dma_start(D.att[ds(HD * h, HD), 512 * c:512 * c + 512], og[s][0:HD]).then_inc(ogst[s], 16)
                        wait_apart(pool, oea, 2 * NC * i + u + 1, made, 9)
                        pool.dma_start(D.lsum[ds(h, 1), 512 * c:512 * c + 512], og[s][HD:HR]).then_inc(ogst[s], 16)
                    elif w[0] == "LD":
                        s = w[1]
                        if not (first and s == 0):
                            wait_apart(pool, pv, NS * i + s * (NS // 2), made, 9)
                            nc.gpsimd.memset(Q2[1 - s][HD:HR].bitcast(F32), 1.0).then_inc(onesd, 1)
                            pool.wait_ge(onesd, 2 * i + 2 + s)

            iterations(pool, run)
            run(B, tail, False)
            pool.wait_ge(ogst[0], 32 * NC * B)
            pool.wait_ge(ogst[1], 32 * NC * B)

        @block.tensor
        def _(pe):
            def run(i, seq, first):
                for w in seq:
                    if w[0] == "M":
                        _, u, j, seg, m = w
                        c, s = u % NC, u // NC
                        if j == 0 and seg == 0 and c == 0:
                            pe.wait_ge(ld[s], 16 * NLD * (i + 1))
                            pe.wait_ge(onesd, 2 if first else (2 * i + 1 if s == 0 else 2 * i + 2))
                        if m < 2:
                            pe.wait_ge(mread, NS * i)
                        else:
                            pe.wait_ge(mread, NS * i + m - 1)
                        t = 4 * c + j
                        wd = 512 if seg < c else (j + 1) * P
                        last = nc.tensor.matmul(MX[m % 2][:, 0:wd], Q2[s][0:HR, t * P:(t + 1) * P], KM[s][0:HR, seg * 512:seg * 512 + wd],
                                                start=True, stop=seg < c)
                        if seg == c:
                            last = nc.tensor.matmul(MX[m % 2][:, j * P:(j + 1) * P], identr[:], maskr[:], start=False, stop=True)
                        last.then_inc(mdone, 1)
                    elif w[0] == "MR":
                        u = w[1]
                        pe.wait_ge(mnd, 2 * NC * i + u + 1)
                        pe.wait_ge(rowd, 2 * NC * i + u)
                        for j in range(4):
                            last = nc.tensor.matmul(MR[0:1, j * P:(j + 1) * P], mneg[:, u % 2, j:j + 1], C.ident[:], start=True, stop=True)
                        last.then_inc(mrd, 1)
                    elif w[0] == "QK":
                        _, u, kb, n = w
                        c, s = u % NC, u // NC
                        j = max(0, kb - 4 * c)
                        q0, wd = 512 * c + P * j, 512 - P * j
                        pe.wait_ge(ex, NS * i + max(0, n - 1))
                        if kb == 0:
                            pe.wait_ge(rowd, 2 * NC * i + u + 1)
                        ks = slice(kb * P, (kb + 1) * P)
                        nc.tensor.matmul(ST[n % 2][:, 0:wd], K1[s][:, ks], Q1[s][:, q0:q0 + wd], start=True, stop=False)
                        diagonal = kb >= 4 * c
                        last = nc.tensor.matmul(ST[n % 2][:, 0:wd], K2[s][:, ks], Q2[s][:, q0:q0 + wd], start=False, stop=not diagonal)
                        if diagonal:
                            last = nc.tensor.matmul(ST[n % 2][:, 0:P], maskr[:], identr[:], start=False, stop=True)
                        last.then_inc(qk, 1)
                    elif w[0] == "PV":
                        _, u, kb, n = w
                        c, s = u % NC, u // NC
                        j = max(0, kb - 4 * c)
                        pe.wait_ge(ex, NS * i + n + 1)
                        if kb == 0:
                            pe.wait_ge(oed, 2 * NC * i + u)
                            pe.wait_ge(oea, 2 * NC * i + u)
                        nc.tensor.matmul(O[0:HR, P * j:512], V[s][:, kb, :], W[n % 3][:, 0:512 - P * j],
                                         start=(kb == 0), stop=(kb == 4 * c + 3)).then_inc(pv, 1)
                    elif w[0] == "SA":
                        pe.wait_ge(smaxd, i)
                        nc.tensor.transpose(CV[0:H, 0, 0:P], smx[:], C.ident[:]).then_inc(sall, 1)
                    elif w[0] == "SC":
                        pe.wait_ge(sdiag, i)
                        nc.tensor.matmul(CV[:, 1, 0:H], onesh[:], smd[:], start=True, stop=True).then_inc(sspread, 1)
                    elif w[0] == "SX":
                        pe.wait_ge(sl4, i)
                        nc.tensor.matmul(CV[:, 0, 0:1], l4[:].rearrange("p l r -> p (l r)"), C.onescol[:], start=True, stop=True).then_inc(slmm, 1)
                    elif w[0] in ("VG", "VN"):
                        r = w[1] if w[0] == "VG" else PG // 4
                        if r == 0:
                            pe.wait_ge(sexp, i)
                            pe.wait_ge(srcp, i)
                        if w[0] == "VG":
                            for g in range(4):
                                pe.wait_ge(v_in[g], 16 * ((PG // 4) * (i - 1) + r + 1))
                        else:
                            pe.wait_ge(vnew_in, 16 * i)
                        for half in range(z.D // 512):
                            for g in range(4 if w[0] == "VG" else 1):
                                src = vp[:, g] if w[0] == "VG" else vnew[:]
                                last = nc.tensor.matmul(CV[32 * g:32 * g + 32, half, :], sw[:, 4 * r + g, :],
                                                        src[:, 512 * half:512 * half + 512], start=(r == 0),
                                                        stop=(r == (PG // 4 if g == 0 else PG // 4 - 1)))
                        last.then_inc(vdone, 1)
                    elif w[0] == "VA":
                        pe.wait_ge(vmask, i)
                        for k in range(z.KB):
                            last = nc.tensor.matmul(CV[:, 0, k:k + 1], cm[:, k * P:(k + 1) * P], C.onescol[:], start=True, stop=True)
                        last.then_inc(vatt, 1)

            pe.wait_ge(made, 9)
            pe.wait_ge(dvm, 2)
            iterations(pe, run)
            run(B, tail, False)

        @block.scalar
        def _(act):
            def run(i, seq, first):
                for w in seq:
                    if w[0] == "QK":
                        _, u, kb, n = w
                        c = u % NC
                        wd = 512 - P * max(0, kb - 4 * c)
                        wait_apart(act, qk, NS * i + n + 1, made, 3)
                        nc.scalar.activation(W[n % 3][:, 0:wd], ST[n % 2][:, 0:wd], ACT.Exp,
                                             bias=C.nckt[:, kb, ds(2 * i + u // NC, 1)]).then_inc(ex, 1)
                    elif w[0] == "MR":
                        u = w[1]
                        c, s = u % NC, u // NC
                        act.wait_ge(mrd, 2 * NC * i + u + 1)
                        nc.scalar.activation(Q2[s][HD:HR, 512 * c:512 * c + 512], MR[0:1, :], ACT.Copy).then_inc(rowd, 1)
                    elif w[0] == "OE":
                        u = w[1]
                        act.wait_ge(pv, NS * i + sum(4 * (x % NC + 1) for x in range(u + 1)))
                        act.wait_ge(ogst[u % 2], 32 * (NC * i + u // 2))
                        nc.scalar.activation(og[u % 2][HD:HR, :], O[HD:HR, :], ACT.Copy).then_inc(oea, 1)
                    elif w[0] == "SE":
                        act.wait_ge(ssub, i)
                        nc.scalar.activation(sw[:, :, 0:H].rearrange("p g h -> p h g"), sd[:], ACT.Exp).then_inc(sexp, 1)

            act.wait_ge(made, 3)
            iterations(act, run)
            run(B, tail, False)

        @block.vector
        def _(dve):
            def run(i, seq, first):
                for w in seq:
                    if w[0] == "M":
                        _, u, j, seg, m = w
                        wd = 512 if seg < u % NC else (j + 1) * P
                        dve.wait_ge(mdone, NS * i + m + 1)
                        nc.vector.reduce_max(mx[:, u % 2, j, seg:seg + 1], MX[m % 2][:, 0:wd], AX.X).then_inc(mread, 1)
                    elif w[0] == "MN":
                        u = w[1]
                        dve.wait_ge(mread, NS * i + sum(4 * (x % NC + 1) for x in range(u + 1)))
                        nc.vector.tensor_reduce(mneg[:, u % 2, :], mx[:, u % 2, :, 0:u % NC + 1], AX.X, ALU.max, negate=True).then_inc(mnd, 1)
                    elif w[0] == "OE":
                        u = w[1]
                        c, s = u % NC, u // NC
                        dve.wait_ge(pv, NS * i + sum(4 * (x % NC + 1) for x in range(u + 1)))
                        dve.wait_ge(ogst[u % 2], 32 * (NC * i + u // 2))
                        nc.vector.tensor_tensor(og[u % 2][0:HD, :], O[0:HD, :], SG[s][:, 512 * c:512 * c + 512], ALU.mult).then_inc(oed, 1)
                    elif w[0] == "KM":
                        g = w[1]
                        if g < PG:
                            dve.wait_ge(k_in[g % 4], 16 * ((PG // 4) * i + g // 4 + 1))
                        else:
                            dve.wait_ge(knew_in, 16 * (i + 1))
                        if g == 0:
                            dve.wait_ge(qb_in, 16 * (i + 1))
                        dve.wait_ge(kred, PX * i + g)
                        nc.vector.tensor_tensor(prod[:], kp[:, g % 4] if g < PG else knew[:], qb[:], ALU.mult).then_inc(kmul, 1)
                    elif w[0] == "KR":
                        g = w[1]
                        dve.wait_ge(kmul, PX * i + g + 1)
                        nc.vector.tensor_reduce(sc[:, :, g], prod[:].rearrange("p (h d) -> p h d", d=HD), AX.X, ALU.add).then_inc(kred, 1)
                    elif w[0] == "SD":
                        dve.wait_ge(kred, PX * i + PX)
                        if not first:
                            dve.wait_ge(sexp, i)
                        nc.vector.tensor_tensor(sd[:], sc[:], C.decay[:, ds(i, 1)].rearrange("p o h g -> p (o h) g"), ALU.add).then_inc(sdd, 1)
                    elif w[0] == "SM":
                        dve.wait_ge(sdd, i)
                        nc.vector.reduce_max(smx[:], sd[:], AX.X).then_inc(smaxd, 1)
                    elif w[0] == "SB":
                        dve.wait_ge(sall, i)
                        nc.vector.reduce_max(smh[:], CV[0:H, 0, 0:P], AX.X).then_inc(smhd, 1)
                        dve.wait_ge(smhd, i)
                        nc.vector.tensor_scalar(smd[:], C.ident[0:H, 0:H], smh[:], None, ALU.mult).then_inc(sdiag, 1)
                    elif w[0] == "SS":
                        dve.wait_ge(sspread, i)
                        nc.vector.tensor_tensor(sd[:], sd[:], CV[:, 1, 0:H].rearrange("p (h o) -> p h o", o=1).broadcast_to([P, H, PX]),
                                                ALU.subtract).then_inc(ssub, 1)
                    elif w[0] == "SL":
                        dve.wait_ge(sexp, i)
                        nc.vector.reduce_sum(l4[:, 0, :], sw[:].rearrange("p g r -> p r g"), AX.X).then_inc(sl1, 1)
                        dve.wait_ge(sl1, i)
                        nc.vector.tensor_copy(l4[:, 1:4, :], l4[:, 0:1, :].broadcast_to([P, 3, 32])).then_inc(sl4, 1)
                    elif w[0] == "SR":
                        dve.wait_ge(slmm, i)
                        nc.vector.tensor_scalar(rl[:, 0:1], CV[:, 0, 0:1], 1e-30, None, ALU.max).then_inc(rlw, 1)
                        dve.wait_ge(rlw, i)
                        nc.vector.reciprocal(rl[:, 1:2], rl[:, 0:1]).then_inc(srcp, 1)
                    elif w[0] == "VM":
                        dve.wait_ge(vdone, VI * i)
                        nc.vector.scalar_tensor_tensor(out=cm[:], in0=CV[:].rearrange("p a b -> p (a b)"), scalar=rl[:, 1:2],
                                                       in1=headmask[:], op0=ALU.mult, op1=ALU.mult).then_inc(vmask, 1)
                    elif w[0] == "VC":
                        dve.wait_ge(vatt, i)
                        nc.vector.tensor_copy(atts[:, :, ds(i - 1, 1)].rearrange("p k o -> p (k o)"), CV[:, 0, 0:z.KB]).then_inc(vcopy, 1)

            dve.wait_ge(masked, 3)
            nc.vector.tensor_copy(maskr[:], maskf[:]).then_inc(dvm, 1)
            nc.vector.tensor_copy(identr[:], C.ident[:]).then_inc(dvm, 1)
            dve.wait_ge(masked, 11)
            iterations(dve, run)
            run(B, tail, False)
            dve.wait_ge(sgs_in, 16)
            dve.wait_ge(vcopy, B)
            nc.vector.tensor_tensor(atts[:], atts[:], sgs[:], ALU.mult).then_inc(fin, 2)


class Names:
    pass


def hybrid_step(nc, a, out):
    z = Shapes(a)
    C, D = Names(), Names()

    def dram(n, shape, dt=F32):
        return nc.dram_tensor(n, shape, dt, kind="Internal").ap()

    D.mixed = dram("mixed", (z.D, z.TS))
    D.x1 = dram("x1", (z.TS, z.D))
    D.qh, D.ql, D.kh, D.kl = (dram(n, (z.D, z.T)) for n in ("qh", "ql", "kh", "kl"))
    D.sg = dram("sg", (z.D, z.TS))
    D.qs = dram("qs", (z.B, z.D))
    D.nck = dram("nck", (z.H, z.T))
    D.att = dram("att", (z.D, z.TS))
    D.lsum = dram("lsum", (z.H, z.TS))

    def x0_of(col, rows):
        return a["x_prompt"][0, ds(col, rows), :] if rows == P else a["x_sample"][:, 0, :]

    def x1_of(col, rows):
        return D.x1[ds(col, rows), :]

    def y_of(col, rows):
        return out["y_prompt"][0, ds(col, rows), :] if rows == P else out["y_sample"][:, 0, :]

    with ExitStack() as common:
        S = Stage(nc, common, "c")
        C.ident = S.sb("ident", [P, P])
        C.onescol = S.sb("onescol", [P, 1])
        C.eps = S.sb("eps", [P, 1])
        C.qg, C.kg = S.sb("qg", [P, 1]), S.sb("kg", [P, 1])
        C.bf = S.sb("bf", [z.H, 1])
        C.nckt = S.sb("nckt", [P, z.NT, z.H])
        with ExitStack() as both:
            S = Stage(nc, both, "x")
            C.pairsum = S.sb("pairsum", [P, P])
            xh = S.sb("xh", [P, z.KB, z.TP], F32R)
            xl = S.sb("xl", [P, z.KB, z.TP], F32R)
            with ExitStack() as first:
                S = Stage(nc, first, "c0")
                C.gv, C.bs = S.sb("gv", [P, z.AW]), S.sb("bs", [P, z.AW])
                C.wst = S.sb("wst", [P, z.G, P])
                C.w00 = S.sb("w00", [z.B, z.G, z.B])
                C.convw, C.convb = S.sb("convw", [P, z.G, z.TAPS]), S.sb("convb", [P, z.G])
                C.br, C.bi, C.lsc = S.sb("br", [P, z.G]), S.sb("bi", [P, z.G]), S.sb("lsc", [P, z.G])
                C.stc = S.sb("stc", [P, z.G, 3 * z.B])
                C.h0 = S.sb("h0", [P, z.G, z.B])
                setup(nc, z, a, C)
                tiles_stage(nc, z, C, "n0", x0_of, norm_g=a["norm0_g"], xh=xh, xl=xl)
                layer0(nc, z, a, C, xh, xl, D.mixed, out)
            tiles_stage(nc, z, C, "o0", x0_of, norm_g=a["norm1_g"], xh=xh, xl=xl, mix=D.mixed, w_out=a["w_out0"], x_out=x1_of)
            project1(nc, z, a, C, xh, xl, D, out)
        with ExitStack() as second:
            S = Stage(nc, second, "c1")
            C.decay = S.sb("decay", [P, z.B, z.H, z.PX])
            past(nc, z, a, C, out)
            attention(nc, z, a, C, D, out)
        tiles_stage(nc, z, C, "o1", x1_of, mix=D.att, w_out=a["w_out1"], x_out=y_of, lsum=D.lsum)


def kernel(**inputs):
    import numpy as _np
    import concourse.bacc as _bacc
    from concourse import mybir as _mybir
    from concourse.bass_utils import run_bass_kernel_spmd as _run

    nc = _bacc.Bacc("TRN2", target_bir_lowering=False, num_devices=1)
    arrays, a, out = {}, {}, {}
    for name, value in inputs.items():
        v = _np.ascontiguousarray(value)
        arrays[f"in_{name}_dram"] = v
        a[name] = nc.dram_tensor(f"in_{name}_dram", v.shape, _mybir.dt.from_np(v.dtype), kind="ExternalInput").ap()
    (_, T, D), B = inputs["x_prompt"].shape, inputs["x_sample"].shape[0]
    K, W = inputs["state_lru_conv"].shape[1:]
    H, HD = inputs["cache_k"].shape[2:]
    shapes = [("y_prompt", (1, T, D)), ("y_sample", (B, 1, D)), ("lru_conv_prompt", (1, K, W)), ("lru_h_prompt", (1, W)),
              ("k_prompt", (1, T, H, HD)), ("v_prompt", (1, T, H, HD)), ("logf_prompt", (1, T, H)),
              ("gmlp_v_sample", (B, 1, W)), ("lru_conv_sample", (B, K, W)), ("lru_h_sample", (B, W)),
              ("k_sample", (B, 1, H, HD)), ("v_sample", (B, 1, H, HD)), ("logf_sample", (B, 1, H))]
    for name, shape in shapes:
        out[name] = nc.dram_tensor(f"out_{name}_dram", shape, _mybir.dt.float32, kind="ExternalOutput").ap()
    with nc.allow_non_contiguous_dma(reason="small parameters by feature"):
        hybrid_step(nc, a, out)
    r = _run(nc, [arrays], core_ids=[0])
    return tuple(r.results[0][f"out_{name}_dram"] for name, _ in shapes)
```
